# Optimizing a Trainium2 kernel written in Bass

```python
import numpy as np
import jax
import jax.numpy as jnp
from jax import lax

D_MODEL = 2048
BATCH = 1
SEQ = 256
DEPTH = 1

HEAD_DIM = 128
N_HEADS = D_MODEL // HEAD_DIM
MOBA_HEADS = N_HEADS // 2
NSA_HEADS = N_HEADS - MOBA_HEADS
NSA_KV_GROUPS = 2
NSA_REP = NSA_HEADS // NSA_KV_GROUPS
MOBA_WIDTH = MOBA_HEADS * HEAD_DIM
NSA_WIDTH = NSA_HEADS * HEAD_DIM
NSA_KV_WIDTH = NSA_KV_GROUPS * HEAD_DIM
NSA_N_GATES = 3 * NSA_HEADS
IN_COLS = 4 * MOBA_WIDTH + 2 * NSA_WIDTH + 6 * NSA_KV_WIDTH + NSA_N_GATES
MOBA_BLOCK = 256
MOBA_TOPK = 3
MOBA_Q_CHUNK = 32
CMP_BLOCK = 32
CMP_STRIDE = 16
CMP_HIDDEN = 2 * HEAD_DIM
SEL_BLOCK = 64
SEL_TOPK = 8
WINDOW = 512
NSA_Q_CHUNK = 64
ROPE_THETA = 10000.0
EPS = 1e-6

kernel_name = 'hybrid_moba_nsa_layer'

def _split_points():
    sizes = [MOBA_WIDTH] * 4 + [NSA_WIDTH] + [NSA_KV_WIDTH] * 6 + [NSA_N_GATES, NSA_WIDTH]
    return [int(v) for v in np.cumsum(sizes)[:-1]]

def rmsnorm(x, g):
    xf = x.astype(jnp.float32)
    y = xf * lax.rsqrt(jnp.mean(xf * xf, axis=-1, keepdims=True) + EPS)
    return (y * g.astype(jnp.float32)).astype(x.dtype)

def rope_tables(positions):
    inv_freq = 1.0 / (ROPE_THETA ** (jnp.arange(0, HEAD_DIM, 2, dtype=jnp.float32) / HEAD_DIM))
    ang = positions.astype(jnp.float32)[..., None] * inv_freq
    return jnp.cos(ang), jnp.sin(ang)

def apply_rope(x, cos, sin):
    c = cos[:, :, None, :]
    s = sin[:, :, None, :]
    x1, x2 = jnp.split(x.astype(jnp.float32), 2, axis=-1)
    return jnp.concatenate([x1 * c - x2 * s, x2 * c + x1 * s], axis=-1).astype(x.dtype)

def masked_softmax(s, mask):
    s = jnp.where(mask, s, -jnp.inf)
    m = jnp.max(s, axis=-1, keepdims=True)
    m = jnp.where(jnp.isfinite(m), m, 0.0)
    e = jnp.where(mask, jnp.exp(s - m), 0.0)
    return e / jnp.maximum(jnp.sum(e, axis=-1, keepdims=True), 1e-30)

def moba_attention(q, k, v):
    B, H, S, dh = q.shape
    n_blk = -(-S // MOBA_BLOCK)
    pad = n_blk * MOBA_BLOCK - S
    kp = jnp.pad(k, ((0, 0), (0, 0), (0, pad), (0, 0)))
    vp = jnp.pad(v, ((0, 0), (0, 0), (0, pad), (0, 0)))
    kb = kp.reshape(B, H, n_blk, MOBA_BLOCK, dh)
    vb = vp.reshape(B, H, n_blk, MOBA_BLOCK, dh)
    k_mean = jnp.mean(kb.astype(jnp.float32), axis=3)
    k_top = min(MOBA_TOPK, n_blk - 1)
    scale = dh ** -0.5
    b_ix = jnp.arange(B)[:, None, None, None]
    h_ix = jnp.arange(H)[None, :, None, None]
    blk_ix = jnp.arange(n_blk)
    C = MOBA_Q_CHUNK

    def chunk(c0):
        qc = lax.dynamic_slice_in_dim(q, c0, C, axis=2)
        q_pos = c0 + jnp.arange(C)
        own = c0 // MOBA_BLOCK
        k_own = lax.dynamic_slice_in_dim(kp, own * MOBA_BLOCK, MOBA_BLOCK, axis=2)
        v_own = lax.dynamic_slice_in_dim(vp, own * MOBA_BLOCK, MOBA_BLOCK, axis=2)
        own_pos = own * MOBA_BLOCK + jnp.arange(MOBA_BLOCK)
        s_own = jnp.einsum('bhqd,bhkd->bhqk', qc, k_own).astype(jnp.float32) * scale
        m_own = jnp.broadcast_to(own_pos[None, :] <= q_pos[:, None], s_own.shape)
        if k_top == 0:
            p = masked_softmax(s_own, m_own).astype(v.dtype)
            return jnp.einsum('bhqk,bhkd->bhqd', p, v_own)
        gate = jnp.einsum('bhqd,bhnd->bhqn', qc.astype(jnp.float32), k_mean)
        fully_past = (blk_ix[None, :] + 1) * MOBA_BLOCK <= q_pos[:, None]
        gate = jnp.where(fully_past, gate, -jnp.inf)
        g_val, g_idx = lax.top_k(gate, k_top)
        k_sel = kb[b_ix, h_ix, g_idx]
        v_sel = vb[b_ix, h_ix, g_idx]
        s_sel = jnp.einsum('bhqd,bhqnld->bhqnl', qc, k_sel).astype(jnp.float32) * scale
        m_sel = jnp.broadcast_to(jnp.isfinite(g_val)[..., None], s_sel.shape)
        n_sel = k_top * MOBA_BLOCK
        s_all = jnp.concatenate([s_sel.reshape(B, H, C, n_sel), s_own], axis=-1)
        m_all = jnp.concatenate([m_sel.reshape(B, H, C, n_sel), m_own], axis=-1)
        p = masked_softmax(s_all, m_all).astype(v.dtype)
        p_sel = p[..., :n_sel].reshape(B, H, C, k_top, MOBA_BLOCK)
        return (jnp.einsum('bhqnl,bhqnld->bhqd', p_sel, v_sel)
                + jnp.einsum('bhqk,bhkd->bhqd', p[..., n_sel:], v_own))

    out = lax.map(chunk, jnp.arange(S // C) * C)
    return out.transpose(1, 2, 0, 3, 4).reshape(B, H, S, dh)

def compress_tokens(kv, pe, w1, w2):
    B, S, G, dh = kv.shape
    n_seg = S // CMP_STRIDE
    r = CMP_BLOCK // CMP_STRIDE
    n_cmp = n_seg - r + 1
    seg = kv.reshape(B, n_seg, CMP_STRIDE, G, dh)
    blocks = jnp.concatenate([seg[:, i:i + n_cmp] for i in range(r)], axis=2)
    blocks = blocks + pe[None, None, :, None, :]
    flat = blocks.transpose(0, 3, 1, 2, 4).reshape(B, G, n_cmp, CMP_BLOCK * dh)
    return jax.nn.silu(flat @ w1) @ w2

def cmp_to_sel_overlap(n_cmp, n_sel_blk):
    cs = np.arange(n_cmp)[:, None] * CMP_STRIDE
    ss = np.arange(n_sel_blk)[None, :] * SEL_BLOCK
    ov = (cs < ss + SEL_BLOCK) & (cs + CMP_BLOCK > ss)
    return jnp.asarray(ov.astype(np.float32))

def nsa_attention(q_rot, q_raw, k_c, v_c, k_s, v_s, k_w, v_w, gates):
    B, G, R, S, dh = q_rot.shape
    scale = dh ** -0.5
    pos = jnp.arange(S)
    n_cmp = k_c.shape[2]
    s_c = jnp.einsum('bgrqd,bgnd->bgrqn', q_raw, k_c).astype(jnp.float32) * scale
    cmp_end = jnp.arange(n_cmp) * CMP_STRIDE + CMP_BLOCK - 1
    p_c = masked_softmax(s_c, cmp_end[None, :] <= pos[:, None])
    o_c = jnp.einsum('bgrqn,bgnd->bgrqd', p_c.astype(v_c.dtype), v_c)
    n_blk = S // SEL_BLOCK
    imp = jnp.einsum('bgrqn,nj->bgqj', p_c, cmp_to_sel_overlap(n_cmp, n_blk))
    blk = jnp.arange(n_blk)[None, :]
    own = (pos // SEL_BLOCK)[:, None]
    forced = (blk == 0) | (blk == own) | (blk == own - 1)
    future = blk * SEL_BLOCK > pos[:, None]
    score = jnp.where(future, -jnp.inf, jnp.where(forced, jnp.inf, imp))
    n_top = min(SEL_TOPK, n_blk)
    s_val, s_idx = lax.top_k(score, n_top)
    s_ok = s_val > -jnp.inf
    ksb = k_s.reshape(B, G, n_blk, SEL_BLOCK, dh)
    vsb = v_s.reshape(B, G, n_blk, SEL_BLOCK, dh)
    kwp = jnp.pad(k_w, ((0, 0), (0, 0), (WINDOW, 0), (0, 0)))
    vwp = jnp.pad(v_w, ((0, 0), (0, 0), (WINDOW, 0), (0, 0)))
    b_ix = jnp.arange(B)[:, None, None, None]
    g_ix = jnp.arange(G)[None, :, None, None]
    C = NSA_Q_CHUNK
    n_keys = n_top * SEL_BLOCK

    def chunk(c0):
        qc = lax.dynamic_slice_in_dim(q_rot, c0, C, axis=3)
        q_pos = c0 + jnp.arange(C)
        idx = lax.dynamic_slice_in_dim(s_idx, c0, C, axis=2)
        ok = lax.dynamic_slice_in_dim(s_ok, c0, C, axis=2)
        k_sel = ksb[b_ix, g_ix, idx]
        v_sel = vsb[b_ix, g_ix, idx]
        s_s = jnp.einsum('bgrqd,bgqnld->bgrqnl', qc, k_sel).astype(jnp.float32) * scale
        key_pos = idx[..., None] * SEL_BLOCK + jnp.arange(SEL_BLOCK)
        m_s = ok[..., None] & (key_pos <= q_pos[None, None, :, None, None])
        p_s = masked_softmax(s_s.reshape(B, G, R, C, n_keys), m_s.reshape(B, G, 1, C, n_keys))
        p_s = p_s.reshape(B, G, R, C, n_top, SEL_BLOCK).astype(v_s.dtype)
        o_s = jnp.einsum('bgrqnl,bgqnld->bgrqd', p_s, v_sel)
        k_win = lax.dynamic_slice_in_dim(kwp, c0, WINDOW + C, axis=2)
        v_win = lax.dynamic_slice_in_dim(vwp, c0, WINDOW + C, axis=2)
        w_pos = c0 - WINDOW + jnp.arange(WINDOW + C)
        m_w = ((w_pos[None, :] <= q_pos[:, None]) & (w_pos[None, :] > q_pos[:, None] - WINDOW)
               & (w_pos[None, :] >= 0))
        s_w = jnp.einsum('bgrqd,bgkd->bgrqk', qc, k_win).astype(jnp.float32) * scale
        p_w = masked_softmax(s_w, m_w).astype(v_w.dtype)
        o_w = jnp.einsum('bgrqk,bgkd->bgrqd', p_w, v_win)
        return o_s, o_w

    o_s, o_w = lax.map(chunk, jnp.arange(S // C) * C)
    o_s = o_s.transpose(1, 2, 3, 0, 4, 5).reshape(B, G, R, S, dh)
    o_w = o_w.transpose(1, 2, 3, 0, 4, 5).reshape(B, G, R, S, dh)
    return gates[..., 0:1] * o_c + gates[..., 1:2] * o_s + gates[..., 2:3] * o_w

def hybrid_layer(x, cos, sin, w_in, g_norm, pe_ck, pe_cv, w_ck1, w_ck2, w_cv1, w_cv2,
                 g_out_moba, g_out_nsa, w_out):
    B, S, _ = x.shape
    G = NSA_KV_GROUPS
    h = rmsnorm(x, g_norm)
    proj = jnp.einsum('bsd,de->bse', h, w_in)
    (m_q, m_k, m_v, m_z, n_q, n_kc, n_vc, n_ks, n_vs, n_kw, n_vw, n_g, n_z) = jnp.split(
        proj, _split_points(), axis=-1)
    mq = apply_rope(m_q.reshape(B, S, MOBA_HEADS, HEAD_DIM), cos, sin).transpose(0, 2, 1, 3)
    mk = apply_rope(m_k.reshape(B, S, MOBA_HEADS, HEAD_DIM), cos, sin).transpose(0, 2, 1, 3)
    mv = m_v.reshape(B, S, MOBA_HEADS, HEAD_DIM).transpose(0, 2, 1, 3)
    o_moba = moba_attention(mq, mk, mv).transpose(0, 2, 1, 3).reshape(B, S, MOBA_WIDTH)
    y_moba = rmsnorm(o_moba * jax.nn.silu(m_z), g_out_moba)
    nq = n_q.reshape(B, S, NSA_HEADS, HEAD_DIM)
    q_rot = apply_rope(nq, cos, sin).reshape(B, S, G, NSA_REP, HEAD_DIM).transpose(0, 2, 3, 1, 4)
    q_raw = nq.reshape(B, S, G, NSA_REP, HEAD_DIM).transpose(0, 2, 3, 1, 4)
    k_c = compress_tokens(n_kc.reshape(B, S, G, HEAD_DIM), pe_ck, w_ck1, w_ck2)
    v_c = compress_tokens(n_vc.reshape(B, S, G, HEAD_DIM), pe_cv, w_cv1, w_cv2)
    k_s = apply_rope(n_ks.reshape(B, S, G, HEAD_DIM), cos, sin).transpose(0, 2, 1, 3)
    v_s = n_vs.reshape(B, S, G, HEAD_DIM).transpose(0, 2, 1, 3)
    k_w = apply_rope(n_kw.reshape(B, S, G, HEAD_DIM), cos, sin).transpose(0, 2, 1, 3)
    v_w = n_vw.reshape(B, S, G, HEAD_DIM).transpose(0, 2, 1, 3)
    gates = jax.nn.sigmoid(n_g.reshape(B, S, G, NSA_REP, 3)).transpose(0, 2, 3, 1, 4)
    o_nsa = nsa_attention(q_rot, q_raw, k_c, v_c, k_s, v_s, k_w, v_w, gates)
    o_nsa = o_nsa.transpose(0, 3, 1, 2, 4).reshape(B, S, NSA_WIDTH)
    y_nsa = rmsnorm(o_nsa * jax.nn.silu(n_z), g_out_nsa)
    y = jnp.concatenate([y_moba, y_nsa], axis=-1)
    return x + jnp.einsum('bse,ed->bsd', y, w_out)

def setup_inputs(seed: int = 0) -> dict:
    key = jax.random.key(seed)
    ks = jax.random.split(key, 13)
    f32 = jnp.float32

    def nrm(k, shape, fan_in):
        return jax.random.normal(k, shape, f32) * (fan_in ** -0.5)

    x = jax.random.normal(ks[0], (BATCH, SEQ, D_MODEL), f32)
    positions = jnp.broadcast_to(jnp.arange(SEQ, dtype=jnp.int32)[None, :], (BATCH, SEQ))
    w_in = nrm(ks[1], (DEPTH, D_MODEL, IN_COLS), D_MODEL)
    g_norm = 1.0 + 0.01 * jax.random.normal(ks[2], (DEPTH, D_MODEL), f32)
    pe_ck = 0.1 * jax.random.normal(ks[3], (DEPTH, CMP_BLOCK, HEAD_DIM), f32)
    pe_cv = 0.1 * jax.random.normal(ks[4], (DEPTH, CMP_BLOCK, HEAD_DIM), f32)
    w_ck1 = nrm(ks[5], (DEPTH, CMP_BLOCK * HEAD_DIM, CMP_HIDDEN), CMP_BLOCK * HEAD_DIM)
    w_ck2 = nrm(ks[6], (DEPTH, CMP_HIDDEN, HEAD_DIM), CMP_HIDDEN)
    w_cv1 = nrm(ks[7], (DEPTH, CMP_BLOCK * HEAD_DIM, CMP_HIDDEN), CMP_BLOCK * HEAD_DIM)
    w_cv2 = nrm(ks[8], (DEPTH, CMP_HIDDEN, HEAD_DIM), CMP_HIDDEN)
    g_out_moba = 1.0 + 0.01 * jax.random.normal(ks[9], (DEPTH, MOBA_WIDTH), f32)
    g_out_nsa = 1.0 + 0.01 * jax.random.normal(ks[10], (DEPTH, NSA_WIDTH), f32)
    w_out = nrm(ks[11], (DEPTH, D_MODEL, D_MODEL), D_MODEL)
    g_final = 1.0 + 0.01 * jax.random.normal(ks[12], (D_MODEL,), f32)
    return {'x': x, 'positions': positions, 'w_in': w_in, 'g_norm': g_norm,
            'pe_ck': pe_ck, 'pe_cv': pe_cv, 'w_ck1': w_ck1, 'w_ck2': w_ck2,
            'w_cv1': w_cv1, 'w_cv2': w_cv2, 'g_out_moba': g_out_moba,
            'g_out_nsa': g_out_nsa, 'w_out': w_out, 'g_final': g_final}

def reference(x, positions, w_in, g_norm, pe_ck, pe_cv, w_ck1, w_ck2, w_cv1, w_cv2,
              g_out_moba, g_out_nsa, w_out, g_final):
    cos, sin = rope_tables(positions)
    for layer in range(DEPTH):
        x = hybrid_layer(x, cos, sin, w_in[layer], g_norm[layer], pe_ck[layer], pe_cv[layer],
                         w_ck1[layer], w_ck2[layer], w_cv1[layer], w_cv2[layer],
                         g_out_moba[layer], g_out_nsa[layer], w_out[layer])
    return rmsnorm(x, g_final)


_drawn_inputs = setup_inputs


def setup_inputs(seed=0):
    import zlib

    import numpy as np

    out = dict(_drawn_inputs(seed))
    spreads = {}
    factors = {'g_norm': 4.292,
     'pe_ck': 7.078,
     'g_out_moba': 64.0,
     'g_out_nsa': 64.0,
     'g_final': 33.851,
     'pe_cv': 7.803}
    for name, (base, spread) in spreads.items():
        noise = np.random.default_rng([zlib.crc32(name.encode()), seed]).standard_normal(out[name].shape)
        drawn = base * np.exp(spread * noise) if base else spread * noise
        out[name] = jnp.asarray(drawn.astype(out[name].dtype))
    for name, factor in factors.items():
        out[name] = (out[name] * factor).astype(out[name].dtype)
    return out
```

```python
import concourse.bass as bass
from concourse import mybir
from contextlib import ExitStack


S, D, P, HD = 256, 2048, 128, 128
MT = S // P
KT = D // P
NH = 8
HW = NH * HD
CW = 512
UK = 4
UPC = KT // UK
HPC = CW // HD
NG, NGATE = 2, 24
NCMP, CL, CS, CH = 15, 32, 16, 256
SCALE = HD ** -0.5
EPS = 1e-6
NEG = -3.0e38
FLOOR = -1.0e38
HALF = HD // 2

COL_MQ, COL_MK, COL_MV, COL_MZ = 0, HW, 2 * HW, 3 * HW
COL_NQ = 4 * HW
COL_KC = 5 * HW
COL_KS, COL_KW, COL_G = COL_KC + 512, COL_KC + 1024, COL_KC + 1536
COL_NZ = COL_G + NGATE
CHUNKS = [("kc", COL_KC, 0), ("kv", COL_KS, 0), ("kv", COL_KW, 1), ("nq", COL_NQ, 0), ("nq", COL_NQ + CW, 1),
          ("mq", COL_MQ, 0), ("mk", COL_MK, 0), ("mv", COL_MV, 0), ("mq", COL_MQ + CW, 1),
          ("mk", COL_MK + CW, 1), ("mv", COL_MV + CW, 1),
          ("z", COL_MZ, 0), ("z", COL_MZ + CW, 1), ("z", COL_NZ, 2), ("z", COL_NZ + CW, 3)]
NC = len(CHUNKS)
NPROJ = NC * UPC
OUT_UNITS = [(0, 0), (0, 1), (1, 0), (1, 1), (0, 2), (1, 2), (0, 3), (1, 3)] + [(c, g) for c in (2, 3) for g in range(4)]
NSLOT = NPROJ + len(OUT_UNITS)
OUT_DONE = [NPROJ + max(i for i, u in enumerate(OUT_UNITS) if u[0] == c) for c in range(4)]
RAW, SPL = 3, 3

ACT_READS = {"kc": 2, "kv": 2, "nq": 2, "mq": 0, "mk": 0, "mv": 2, "z": 2, "out": 0}
DVE_READS = {"kc": 0, "kv": 4, "nq": 4, "mq": 4, "mk": 4, "mv": 0, "z": 2, "out": 2}
KINDS = [c[0] for c in CHUNKS] + ["out"] * 4
ROPED = ("kv", "nq", "mq", "mk")


def act_reads(i):
    return sum(ACT_READS[k] for k in KINDS[:i + 1])


def dve_reads(i):
    return sum(DVE_READS[k] for k in KINDS[:i + 1])


def rope_sums(i):
    return 2 * sum(k in ROPED for k in KINDS[:i + 1])


Q_ROT, Q_RAW, Q_KS, Q_MQ, Q_MK = 0, 8, 16, [20, 0], [24, 8]


def transpose_rounds():
    out = {}
    for i, (kind, _, n) in enumerate(CHUNKS):
        s = UPC * i + UPC
        if kind == "kc":
            out[s], out[s + 1] = ("kc", 0, i), ("kc", 1, i)
        elif kind == "kv":
            out[s] = ("kv", n, i)
        elif kind == "nq":
            for k, m in ((0, 0), (0, 1), (1, 0), (1, 1)):
                out[s + 2 * k + m] = (("rot", "raw")[k], (n, m), i)
        elif kind in ("mq", "mk"):
            out[s], out[s + 1] = (kind, (n, 0), i), (kind, (n, 1), i)
    return out


ROUNDS = transpose_rounds()
ROUND_NO = {s: n for n, s in enumerate(sorted(ROUNDS))}


def rounds_by(slot):
    return sum(s <= slot for s in ROUNDS)


JOBS = [(20 + 2 * h + b, "nsa", h, b) for h in range(8) for b in range(2)] + \
       [(36 + h, "moba", h, 0) for h in range(4)] + [(42 + h, "moba", 4 + h, 0) for h in range(4)]
JOB_AT = {j[0]: n for n, j in enumerate(JOBS)}
LAST_JOB_SLOT = JOBS[-1][0]


def score_reads(j):
    return sum(3 if JOBS[i][1] == "nsa" else 2 for i in range(j + 1))


def ends_head(j):
    return JOBS[j][1] == "moba" or JOBS[j][3] == 1


def heads_done(j):
    return sum(ends_head(i) for i in range(j + 1))


CK_SLOT = [6, 7, 9, 10, 12, 13, 15, 16]
CK_AT = {s: c for c, s in enumerate(CK_SLOT)}
CK2_SLOT = [12, 18]
GATE_SLOT = 18
Y_ROUNDS = {54: [(0, 0, 0)], 55: [(0, 0, 1)], 56: [(0, 1, 0)], 57: [(0, 1, 1)],
            62: [(1, 0, 0), (1, 0, 1)], 63: [(1, 1, 0), (1, 1, 1)]}
Y_NO = {r: n for n, r in enumerate(r for s in sorted(Y_ROUNDS) for r in Y_ROUNDS[s])}

INV_2PI = 0.15915494309189535
MAGIC = 12582912.0
C1 = 6.28125
C2 = 0.0019350051879882812
C3 = 6.283185307179586 - C1 - C2
PI = 3.1415925


def build_layer(nc, x, positions, inv_freq, w_in, g_norm, pe_ck, pe_cv, w_ck1, w_ck2, w_cv1, w_cv2,
                g_out_moba, g_out_nsa, w_out, g_final, out):
    F32, F32R, BF16, I32 = mybir.dt.float32, mybir.dt.float32r, mybir.dt.bfloat16, mybir.dt.int32
    ALU, ACT = mybir.AluOpType, mybir.ActivationFunctionType

    with ExitStack() as ctx:
        def sb(name, shape, dt=F32):
            return ctx.enter_context(nc.sbuf_tensor(name, shape, dt))

        def sem(name):
            return ctx.enter_context(nc.semaphore(name))

        xo = sb("xo", [P, MT, D])
        xT_hi, xT_lo = sb("xT_hi", [P, KT, S], F32R), sb("xT_lo", [P, KT, S], F32R)
        ymT_hi, ymT_lo = sb("ymT_hi", [P, NH, S], F32R), sb("ymT_lo", [P, NH, S], F32R)
        w_raw = sb("w_raw", [P, RAW, UK, CW])
        w_hi, w_lo = sb("w_hi", [P, SPL, UK, CW], F32R), sb("w_lo", [P, SPL, UK, CW], F32R)
        Q = sb("Q", [P, 28, S])
        acc = Q[:, 0:16, :].rearrange("p a b -> p (a b)").rearrange("p (m d) -> p m d", m=MT)
        g_fin = Q[:, 16:24, :].rearrange("p a b -> p (a b)")
        KV8 = sb("KV8", [P, 2 * D // 2])
        kvpe = KV8[:, :].rearrange("p (v h g t) -> p v h g t", v=2, h=2, g=NG)
        mv = KV8[:, :].rearrange("p (m c) -> p m c", m=MT)
        nv = sb("nv", [P, 2, MT, 2 * HD])
        rope_a, rope_b = sb("rope_a", [P, MT, CW]), sb("rope_b", [P, MT, CW])
        raw_e = sb("raw_e", [P, MT, CW])
        junk = raw_e[:, :, :].rearrange("p m c -> p (m c)").bitcast(BF16)
        prob = sb("prob", [P, 2, 400])
        w2 = prob[:, :, :].rearrange("p a b -> p (a b)")[:, 0:4 * HD].rearrange("p (v t d) -> p v t d", v=2, t=2)
        pT = sb("pT", [P, 2, 512])
        trig = pT[:, 0, :].rearrange("p (a c) -> p a c", a=4)
        crows = pT[0:96, 1, 0:P]
        ident = sb("ident", [P, P])
        mask = sb("mask", [P, 3 * P + 2 * NCMP + 2])
        ccols = sb("ccols", [P, 96])
        invf, pos_i, pos_f = sb("invf", [P, HALF]), sb("pos_i", [P, MT], I32), sb("pos_f", [P, MT])
        rope_c, rope_s = sb("rope_c", [P, MT, HD]), sb("rope_s", [P, MT, HD])
        ssx, rstd, nrstd = sb("ssx", [P, MT]), sb("rstd", [P, MT]), sb("nrstd", [P, MT])
        half_c = sb("half_c", [P, MT])
        mx, sums, coef = sb("mx", [P, 2, 4]), sb("sums", [P, 2, 4]), sb("coef", [P, 2, 4])
        nmx = sb("nmx", [P, 2, 4])
        wg, wg_hi, wg_lo = sb("wg", [P, KT, NGATE]), sb("wg_hi", [P, KT, NGATE], F32R), sb("wg_lo", [P, KT, NGATE], F32R)
        gate, gate_j = sb("gate", [P, MT, NGATE]), sb("gate_j", [P, NH, 2, 4])
        hid_e, hidT = sb("hid_e", [P, 2, 32]), sb("hidT", [P, 2, 2, 32])
        kcT, vc = sb("kcT", [P, 32]), sb("vc", [16, NG, HD])
        ssy, rstdy = sb("ssy", [P, 2, MT, 2]), sb("rstdy", [P, 2, MT])
        ssf, ssf1, rstdf = sb("ssf", [P, MT, 4]), sb("ssf1", [P, MT]), sb("rstdf", [P, MT])

        def bank(name):
            return ctx.enter_context(nc.psum_tensor(name, [P, 512], F32))

        proj_b = [[bank(f"proj{i}{m}") for m in range(MT)] for i in range(2)]
        b_s, b_o, b_t, b_p = bank("b_s"), bank("b_o"), bank("b_t"), bank("b_p")
        xbanks = [b_s, b_o, b_t, b_p]

        x_in = [sem(f"x_in{q}") for q in range(4)]
        raw_in = [sem(f"raw_in{i}") for i in range(RAW)]
        ck_in = [sem(f"ck_in{i}") for i in range(2)]
        crow_in, trig_in, wg_in, w2_in = sem("crow_in"), sem("trig_in"), sem("wg_in"), sem("w2_in")
        acc_in, gfin_in, out_in = sem("acc_in"), sem("gfin_in"), sem("out_in")
        ident_ok, consts_ok, pool_step = sem("ident_ok"), sem("consts_ok"), sem("pool_step")
        xlo_done, rstd_ok, rope_sum, y_done = sem("xlo_done"), sem("rstd_ok"), sem("rope_sum"), sem("y_done")
        rstdy_ok, rstdf_ok = sem("rstdy_ok"), sem("rstdf_ok")
        gmul = sem("gmul")
        crows_T, x_round, unit_used, t_round = sem("crows_T"), sem("x_round"), sem("unit_used"), sem("t_round")
        ck_used, ck2_done, gates_done = sem("ck_used"), sem("ck2_done"), sem("gates_done")
        scores_done, pt_done, pv_done, y_round = sem("scores_done"), sem("pt_done"), sem("pv_done"), sem("y_round")
        hi_ready, xhi_done, sq_done, trig_act = sem("hi_ready"), sem("xhi_done"), sem("sq_done"), sem("trig_act")
        act_read, ck_exp, ck2_out, gate_exp = sem("act_read"), sem("ck_exp"), sem("ck2_out"), sem("gate_exp")
        wghi_ok, exp_done, pt_out, y_sq = sem("wghi_ok"), sem("exp_done"), sem("pt_out"), sem("y_sq")
        yhi_done, fin_sq, fin_act = sem("yhi_done"), sem("fin_sq"), sem("fin_act")
        cols_ok, xg_done, lo_ready, dve_read = sem("cols_ok"), sem("xg_done"), sem("lo_ready"), sem("dve_read")
        dve_step, trig_arg, tables_ok = sem("dve_step"), sem("trig_arg"), sem("tables_ok")
        hid_ready, wglo_ok, gates_ok = sem("hid_ready"), sem("wglo_ok"), sem("gates_ok")
        s_read, negmax_ok, prob_ready, o_out = sem("s_read"), sem("negmax_ok"), sem("prob_ready"), sem("o_out")
        y_scaled, yg_done, ylo_done, ssf_ok, fin_dve = sem("y_scaled"), sem("yg_done"), sem("ylo_done"), sem("ssf_ok"), sem("fin_dve")
        t_out = sem("t_out")

        block = ctx.enter_context(nc.Block())

        def unit_src(u):
            if u < NPROJ:
                col, g = CHUNKS[u // UPC][1], u % UPC
                src = w_in[0, g * UK * P:(g + 1) * UK * P, col:col + CW]
            else:
                c, g = OUT_UNITS[u - NPROJ]
                src = w_out[0, g * UK * P:(g + 1) * UK * P, c * CW:(c + 1) * CW]
            return src.rearrange("(k p) c -> p k c", p=P)

        @block.sync
        def _(sp):
            def x_quarter(q):
                sp.dma_start(xo[:, :, q * CW:(q + 1) * CW],
                             x[0, :, q * CW:(q + 1) * CW].rearrange("(m p) c -> p m c", p=P)).then_inc(x_in[q], 16)

            def unit(u):
                if u >= RAW:
                    sp.wait_ge(lo_ready, u - RAW + 1)
                sp.dma_start(w_raw[:, u % RAW], unit_src(u)).then_inc(raw_in[u % RAW], 16)

            def ck_unit(c):
                if c == 0:
                    sp.wait_ge(sq_done, 2)
                    sp.wait_ge(x_round, 8)
                if c >= 2:
                    sp.wait_ge(ck_used, c - 1)
                w = (w_ck1, w_cv1)[c // 4]
                l0 = (c % 4) * 8
                sp.dma_start(xo[:, c % 2, :].rearrange("p (l h) -> p l h", l=8),
                             w[0, l0 * HD:(l0 + 8) * HD, :].rearrange("(l d) h -> d l h", d=HD)).then_inc(ck_in[c % 2], 16)

            x_quarter(0)
            unit(0)
            x_quarter(1)
            x_quarter(2)
            unit(1)
            x_quarter(3)
            unit(2)
            ck_next = 0
            for u in range(RAW, NSLOT):
                unit(u)
                while ck_next < 8 and u >= CK_SLOT[ck_next] and u >= 6:
                    ck_unit(ck_next)
                    ck_next += 1
                if u == 54:
                    sp.wait_ge(scores_done, len(JOBS))
                    sp.dma_start(acc, x[0].rearrange("(m p) c -> p m c", p=P)).then_inc(acc_in, 16)
                if u == 56:
                    sp.dma_start(g_fin, g_final.rearrange("(a d) -> a d", a=1).to_broadcast([P, D])).then_inc(gfin_in, 16)
            for m in range(MT):
                sp.wait_ge((fin_dve, fin_act)[m], 1)
                sp.dma_start(out[0, m * P:(m + 1) * P, :], acc[:, m, :]).then_inc(out_in, 16)
            sp.wait_ge(out_in, 16 * MT)

        @block.gpsimd
        def _(pool):
            steps = [0]

            def link(ins):
                steps[0] += 1
                ins.then_inc(pool_step, 1)
                pool.wait_ge(pool_step, steps[0])

            link(nc.gpsimd.memset(ident[:, :], 0.0))
            nc.gpsimd.affine_select(out=ident[:, :], in_=ident[:, :], compare_op=ALU.not_equal, fill=1.0, base=0,
                                    pattern=[[-1, P]], channel_multiplier=1).then_inc(ident_ok, 1)
            nc.gpsimd.memset(half_c[:, :], -0.5)
            link(nc.gpsimd.memset(mask[:, :], 0.0))
            for c0, n, step, base in ((0, P, -1, 0), (2 * P, P, -1, 0), (3 * P, NCMP, -CS, 1 - CL), (3 * P + 16, NCMP, -CS, P + 1 - CL)):
                nc.gpsimd.affine_select(out=mask[:, c0:c0 + n], in_=mask[:, c0:c0 + n], compare_op=ALU.is_ge, fill=NEG,
                                        base=base, pattern=[[step, n]], channel_multiplier=1).then_inc(consts_ok, 1)
            for r in range(8):
                q, m = r // 2, r % 2
                pool.wait_ge(xhi_done, r + 1)
                nc.gpsimd.tensor_tensor(xT_lo[:, q * UK:(q + 1) * UK, m * P:(m + 1) * P],
                                        rope_a[:, r % 2, :].rearrange("p (k t) -> p k t", k=UK),
                                        xT_hi[:, q * UK:(q + 1) * UK, m * P:(m + 1) * P].bitcast(F32),
                                        ALU.subtract).then_inc(xlo_done, 1)
            pool.wait_ge(sq_done, 2)
            link(nc.gpsimd.tensor_scalar(ssx[:, :], ssx[:, :], 1.0 / D, EPS, ALU.mult, ALU.add))
            nc.gpsimd.tensor_tensor(rstd[:, :], ssx[:, :], half_c[:, :], ALU.pow).then_inc(rstd_ok, 1)
            pool.wait_ge(rstd_ok, 1)
            nc.gpsimd.tensor_scalar(nrstd[:, :], rstd[:, :], -1.0, None, ALU.mult).then_inc(rstd_ok, 1)
            for i, kind in enumerate(KINDS[:NC]):
                if kind in ROPED:
                    w = 2 * HD if kind == "kv" else CW
                    for m in range(MT):
                        pool.wait_ge(dve_read, dve_reads(i - 1) + 2 * (m + 1))
                        nc.gpsimd.tensor_tensor(rope_a[:, m, 0:w], rope_a[:, m, 0:w], rope_b[:, m, 0:w],
                                                ALU.add).then_inc(rope_sum, 1)
                elif kind == "z":
                    n = CHUNKS[i][2]
                    z = (rope_a, rope_b)[n % 2]
                    if n == 0:
                        pool.wait_ge(o_out, 2 * NH)
                    for m in range(MT):
                        pool.wait_ge(dve_read, dve_reads(i - 1) + m + 1)
                        nc.gpsimd.tensor_tensor(xo[:, m, n * CW:(n + 1) * CW], xo[:, m, n * CW:(n + 1) * CW],
                                                z[:, m, :], ALU.mult).then_inc(y_done, 1)
                    if n % 2:
                        h = n // 2
                        pool.wait_ge(y_sq, 4 * (h + 1))
                        link(nc.gpsimd.tensor_tensor(rstdy[:, h, :], ssy[:, h, :, 0], ssy[:, h, :, 1], ALU.add))
                        link(nc.gpsimd.tensor_scalar(rstdy[:, h, :], rstdy[:, h, :], 1.0 / HW, EPS, ALU.mult, ALU.add))
                        nc.gpsimd.tensor_tensor(rstdy[:, h, :], rstdy[:, h, :], half_c[:, :], ALU.pow).then_inc(rstdy_ok, 1)
            pool.wait_ge(gfin_in, 16)
            for c in range(3):
                for m in range(MT):
                    pool.wait_ge(fin_sq, 2 * c + m + 1)
                    nc.gpsimd.tensor_tensor(acc[:, m, c * CW:(c + 1) * CW], acc[:, m, c * CW:(c + 1) * CW],
                                            g_fin[:, c * CW:(c + 1) * CW], ALU.mult).then_inc(gmul, 1)
            pool.wait_ge(ssf_ok, 1)
            link(nc.gpsimd.tensor_scalar(ssf1[:, :], ssf1[:, :], 1.0 / D, EPS, ALU.mult, ALU.add))
            nc.gpsimd.tensor_tensor(rstdf[:, :], ssf1[:, :], half_c[:, :], ALU.pow).then_inc(rstdf_ok, 1)

        @block.tensor
        def _(pe):
            def transpose4(bank_, srcs, done):
                for n, src in enumerate(srcs):
                    last = nc.tensor.transpose(bank_[:, n * P:(n + 1) * P], src, ident[:, :])
                last.then_inc(done, 1)

            def x_round_(r):
                q, m = r // 2, r % 2
                if m == 0:
                    pe.wait_ge(x_in[q], 16)
                if r == 3:
                    pe.wait_ge(cols_ok, 1)
                if r >= 4:
                    pe.wait_ge(xg_done, r - 3)
                transpose4(xbanks[r % 4], [xo[:, m, (q * UK + k) * P:(q * UK + k + 1) * P] for k in range(UK)], x_round)

            def split_products(outs, stat_hi, stat_lo, k0, nk, mov_hi, mov_lo, first, last):
                for m in range(MT):
                    tok = slice(m * P, (m + 1) * P)
                    for k in range(nk):
                        a_hi, a_lo = stat_hi[:, k0 + k, tok], stat_lo[:, k0 + k, tok]
                        nc.tensor.matmul(outs[m], a_hi, mov_hi[:, k, :], start=first and k == 0, stop=False)
                        nc.tensor.matmul(outs[m], a_hi, mov_lo[:, k, :], start=False, stop=False)
                        ins = nc.tensor.matmul(outs[m], a_lo, mov_hi[:, k, :], start=False, stop=last and k == nk - 1)
                return ins

            def unit(u):
                if u < NPROJ:
                    c, g = u // UPC, u % UPC
                    if u < UPC:
                        pe.wait_ge(xlo_done, 2 * u + 2)
                    sh, sl, k0 = xT_hi, xT_lo, g * UK
                else:
                    oc, g = OUT_UNITS[u - NPROJ]
                    c = NC + oc
                    pe.wait_ge(ylo_done, 4 if g < 2 else 2 * g + 2)
                    sh, sl, k0 = (ymT_hi, ymT_lo, g * UK) if g < 2 else (xT_hi, xT_lo, (g - 2) * UK)
                if g == 0 and c >= 2:
                    pe.wait_ge(act_read, act_reads(c - 2))
                    pe.wait_ge(dve_read, dve_reads(c - 2))
                pe.wait_ge(lo_ready, u + 1)
                split_products([proj_b[c % 2][m][:, :] for m in range(MT)], sh, sl, k0, UK,
                               w_hi[:, u % SPL], w_lo[:, u % SPL], g == 0, g == UPC - 1).then_inc(unit_used, 1)

            def round_(slot):
                kind, which, i = ROUNDS[slot]
                no = ROUND_NO[slot]
                if no:
                    pe.wait_ge(t_out, no)
                if kind == "kc":
                    pe.wait_ge(act_read, act_reads(i - 1) + which + 1)
                    srcs = [raw_e[:, which, h * HD:(h + 1) * HD] for h in range(HPC)]
                elif kind == "kv":
                    pe.wait_ge(rope_sum, rope_sums(i))
                    srcs = [rope_a[:, m, g * HD:(g + 1) * HD] for g in range(NG) for m in range(MT)]
                elif kind == "raw":
                    pe.wait_ge(act_read, act_reads(i))
                    srcs = [raw_e[:, which[1], h * HD:(h + 1) * HD] for h in range(HPC)]
                else:
                    pe.wait_ge(rope_sum, rope_sums(i - 1) + which[1] + 1)
                    srcs = [rope_a[:, which[1], h * HD:(h + 1) * HD] for h in range(HPC)]
                transpose4(b_t, srcs, t_round)

            def ck_unit(c):
                kv = c // 4
                if c == 0:
                    pe.wait_ge(t_out, 2)
                if c == 4:
                    pe.wait_ge(hid_ready, 1)
                pe.wait_ge(ck_in[c % 2], 16 * (c // 2 + 1))
                w = xo[:, c % 2, :].rearrange("p (l h) -> p l h", l=8)
                for l8 in range(8):
                    l = (c % 4) * 8 + l8
                    part = kvpe[:, kv, l // CS].rearrange("p g (n l) -> p l g n", l=CS)
                    tok = part[:, l % CS, :, l // CS:l // CS + NCMP]
                    for ht in range(2):
                        dst = (b_s, b_p)[ht][:, kv * 32:kv * 32 + 2 * NCMP].rearrange("p (g n) -> p g n", g=NG)
                        last = nc.tensor.matmul(dst, w[:, l8, ht * P:(ht + 1) * P], tok, start=l == 0, stop=l == CL - 1)
                last.then_inc(ck_used, 1)

            def ck_layer2(kv):
                if kv == 0:
                    pe.wait_ge(w2_in, 32)
                pe.wait_ge(hid_ready, kv + 1)
                if kv:
                    pe.wait_ge(ck2_out, 1)
                if kv == 0:
                    for ht in range(2):
                        last = nc.tensor.matmul(b_o[:, 0:2 * NCMP], w2[:, 0, ht, :], hidT[:, 0, ht, 0:2 * NCMP],
                                                start=ht == 0, stop=ht == 1)
                else:
                    for g in range(NG):
                        for ht in range(2):
                            last = nc.tensor.matmul(b_o[0:NCMP, (g + 1) * HD:(g + 2) * HD],
                                                    hidT[:, 1, ht, g * NCMP:(g + 1) * NCMP], w2[:, 1, ht, :],
                                                    start=ht == 0, stop=ht == 1)
                last.then_inc(ck2_done, 1)

            def gates():
                pe.wait_ge(wglo_ok, 1)
                pe.wait_ge(ck2_out, 2)
                split_products([b_o[:, 384 + m * NGATE:384 + (m + 1) * NGATE] for m in range(MT)], xT_hi, xT_lo, 0, KT,
                               wg_hi[:, :, :], wg_lo[:, :, :], True, True).then_inc(gates_done, 1)

            def scores(j):
                slot, kind, h, b = JOBS[j]
                pe.wait_ge(t_out, rounds_by(slot - 1))
                if j:
                    pe.wait_ge(s_read, score_reads(j - 1))
                if kind == "nsa":
                    if j == 0:
                        pe.wait_ge(ck2_out, 2)
                    qt, kt = Q[:, Q_ROT + h, :], Q[:, Q_KS + 2 * b + h // 4, :]
                else:
                    qt, kt = Q[:, Q_MQ[h // 4] + h % 4, :], Q[:, Q_MK[h // 4] + h % 4, :]
                nc.tensor.matmul(b_s[:, 0:P], qt[:, 0:P], kt[:, 0:P], start=True, stop=True)
                last = nc.tensor.matmul(b_s[:, P:3 * P], qt[:, P:S], kt[:, 0:S], start=True, stop=True)
                if kind == "nsa":
                    last = nc.tensor.matmul(b_s[:, 3 * P:3 * P + NCMP], Q[:, Q_RAW + h, b * P:(b + 1) * P],
                                            kcT[:, (h // 4) * NCMP:(h // 4 + 1) * NCMP], start=True, stop=True)
                last.then_inc(scores_done, 1)

            def prob_T(j):
                pe.wait_ge(prob_ready, j + 1)
                if j:
                    pe.wait_ge(pt_out, j)
                for n in range(3):
                    last = nc.tensor.transpose(b_p[:, n * P:(n + 1) * P], prob[:, j % 2, n * P:(n + 1) * P], ident[:, :])
                if JOBS[j][1] == "nsa":
                    last = nc.tensor.transpose(b_p[0:NCMP, 3 * P:4 * P], prob[:, j % 2, 3 * P:3 * P + NCMP], ident[:, :])
                last.then_inc(pt_done, 1)

            def values(j):
                _, kind, h, b = JOBS[j]
                pe.wait_ge(pt_out, j + 1)
                n = heads_done(j) - 1
                if n:
                    pe.wait_ge(o_out, n)
                else:
                    pe.wait_ge(gates_ok, 1)
                if kind == "moba":
                    pe.wait_ge(act_read, act_reads(7 if h < 4 else 10))
                for m in range(MT):
                    prods = []
                    if kind == "moba":
                        for kt in range(m + 1):
                            prods.append((pT[:, j % 2, (m + kt) * P:(m + kt + 1) * P], mv[:, kt, h * HD:(h + 1) * HD]))
                    else:
                        g = h // 4
                        for br in range(2):
                            jb = j - 1 + br
                            for kt in range(m + 1):
                                prods.append((pT[:, jb % 2, (m + kt) * P:(m + kt + 1) * P], nv[:, br, kt, g * HD:(g + 1) * HD]))
                        jb = j - 1 + m
                        prods.append((pT[0:NCMP, jb % 2, 3 * P:4 * P], vc[0:NCMP, g, :]))
                    for n, (a, v) in enumerate(prods):
                        last = nc.tensor.matmul(b_o[:, m * P:(m + 1) * P], a, v, start=n == 0, stop=n == len(prods) - 1)
                last.then_inc(pv_done, 1)

            def y_round_(r):
                half, hg, m = r
                n = Y_NO[r]
                if half == 0:
                    pe.wait_ge(y_scaled, m + 1)
                    if n == 0:
                        pe.wait_ge(t_out, len(ROUNDS))
                    bank_ = b_t
                    if n:
                        pe.wait_ge(yg_done, n)
                else:
                    pe.wait_ge(y_scaled, 2 + m + 1)
                    bank_ = (b_t, b_s, b_p, b_o)[n - 4]
                    if n == 4:
                        pe.wait_ge(yg_done, 4)
                transpose4(bank_, [xo[:, m, half * HW + (hg * HPC + h) * HD:half * HW + (hg * HPC + h + 1) * HD]
                                   for h in range(HPC)], y_round)

            pe.wait_ge(ident_ok, 1)
            pe.wait_ge(crow_in, 80)
            nc.tensor.transpose(b_p[:, 0:96], crows, ident[0:96, 0:96]).then_inc(crows_T, 1)
            for r in range(4):
                x_round_(r)
            for slot in range(NSLOT):
                unit(slot)
                if slot < 2:
                    x_round_(4 + 2 * slot)
                    x_round_(5 + 2 * slot)
                if slot in ROUNDS:
                    round_(slot)
                if slot in CK_AT:
                    ck_unit(CK_AT[slot])
                if slot in CK2_SLOT:
                    ck_layer2(CK2_SLOT.index(slot))
                if slot == GATE_SLOT:
                    gates()
                if slot - 3 in JOB_AT and ends_head(JOB_AT[slot - 3]):
                    values(JOB_AT[slot - 3])
                if slot - 2 in JOB_AT:
                    prob_T(JOB_AT[slot - 2])
                if slot in JOB_AT:
                    scores(JOB_AT[slot])
                for r in Y_ROUNDS.get(slot, []):
                    y_round_(r)

        @block.scalar
        def _(act):
            def hi(u):
                act.wait_ge(raw_in[u % RAW], 16 * (u // RAW + 1))
                if u >= SPL:
                    act.wait_ge(unit_used, u - SPL + 1)
                nc.scalar.activation(w_hi[:, u % SPL], w_raw[:, u % RAW], ACT.Copy).then_inc(hi_ready, 1)

            def x_hi(r):
                q, m = r // 2, r % 2
                act.wait_ge(xg_done, r + 1)
                nc.scalar.activation(xT_hi[:, q * UK:(q + 1) * UK, m * P:(m + 1) * P],
                                     rope_a[:, r % 2, :].rearrange("p (k t) -> p k t", k=UK), ACT.Copy).then_inc(xhi_done, 1)

            def evac(i):
                kind, _, n = CHUNKS[i]
                act.wait_ge(unit_used, UPC * (i + 1))
                if i == 0:
                    act.wait_ge(rstd_ok, 1)
                if kind == "nq" and n:
                    act.wait_ge(t_round, rounds_by(UPC * i + UPC - 1))
                for m in range(MT):
                    b = proj_b[i % 2][m]
                    if kind in ("kv", "nq"):
                        act.wait_ge(dve_read, dve_reads(i - 1) + 2 * (m + 1))
                    if kind in ("kc", "nq"):
                        nc.scalar.activation(raw_e[:, m, :], b[:, :], ACT.Copy, scale=rstd[:, m:m + 1]).then_inc(act_read, 1)
                    elif kind == "kv":
                        nc.scalar.activation(nv[:, n, m, :], b[:, 2 * HD:4 * HD], ACT.Copy, scale=rstd[:, m:m + 1]).then_inc(act_read, 1)
                    elif kind == "mv":
                        nc.scalar.activation(mv[:, m, n * CW:(n + 1) * CW], b[:, :], ACT.Copy, scale=rstd[:, m:m + 1]).then_inc(act_read, 1)
                    elif kind == "z":
                        z = (rope_a, rope_b)[n % 2]
                        if n >= 2 and m == 0:
                            act.wait_ge(y_done, 2 * (n - 1))
                        if n == 0 and m == 0:
                            act.wait_ge(t_round, len(ROUNDS))
                        nc.scalar.activation(z[:, m, :], b[:, :], ACT.Sigmoid, scale=rstd[:, m:m + 1]).then_inc(act_read, 1)

            def round_out(slot):
                kind, which, _ = ROUNDS[slot]
                if kind == "kc":
                    return
                act.wait_ge(t_round, ROUND_NO[slot] + 1)
                if kind == "kv":
                    dst = Q[:, Q_KS + 2 * which:Q_KS + 2 * which + 2, :]
                    src = b_t[:, :].rearrange("p (g t) -> p g t", g=NG)
                else:
                    n, m = which
                    first = {"rot": Q_ROT + 4 * n, "raw": Q_RAW + 4 * n, "mq": Q_MQ[n], "mk": Q_MK[n]}[kind]
                    dst = Q[:, first:first + HPC, m * P:(m + 1) * P]
                    src = b_t[:, :].rearrange("p (h t) -> p h t", h=HPC)
                nc.scalar.activation(dst, src, ACT.Copy).then_inc(t_out, 1)

            def exps(j):
                act.wait_ge(negmax_ok, j + 1)
                b = j % 2
                for n, (c0, c1) in enumerate(((0, P), (P, 3 * P), (3 * P, 3 * P + NCMP))[:3 if JOBS[j][1] == "nsa" else 2]):
                    last = nc.scalar.activation(prob[:, b, c0:c1], prob[:, b, c0:c1], ACT.Exp, bias=nmx[:, b, n:n + 1],
                                                scale=SCALE, accum_out=sums[:, b, n:n + 1])
                last.then_inc(exp_done, 1)

            def prob_out(j):
                act.wait_ge(pt_done, j + 1)
                last = nc.scalar.activation(pT[:, j % 2, 0:3 * P], b_p[:, 0:3 * P], ACT.Copy)
                if JOBS[j][1] == "nsa":
                    last = nc.scalar.activation(pT[0:NCMP, j % 2, 3 * P:4 * P], b_p[0:NCMP, 3 * P:4 * P], ACT.Copy)
                last.then_inc(pt_out, 1)

            def hidden_exp(kv):
                act.wait_ge(ck_used, 4 * (kv + 1))
                for ht in range(2):
                    last = nc.scalar.activation(hid_e[:, ht, 0:2 * NCMP], (b_s, b_p)[ht][:, kv * 32:kv * 32 + 2 * NCMP], ACT.Exp, scale=-1.0)
                last.then_inc(ck_exp, 1)

            def ck2_evac(kv):
                act.wait_ge(ck2_done, kv + 1)
                if kv == 0:
                    nc.scalar.activation(kcT[:, 0:2 * NCMP], b_o[:, 0:2 * NCMP], ACT.Copy).then_inc(ck2_out, 1)
                else:
                    nc.scalar.activation(vc[0:NCMP, :, :], b_o[0:NCMP, HD:3 * HD].rearrange("p (g d) -> p g d", g=NG),
                                         ACT.Copy).then_inc(ck2_out, 1)

            def y_squares(n):
                for m in range(MT):
                    act.wait_ge(y_done, 2 * n + m + 1)
                    if n + m:
                        act.wait_ge(y_sq, 2 * n + m)
                    nc.scalar.activation(junk[:, 0:CW], xo[:, m, n * CW:(n + 1) * CW], ACT.Square,
                                         accum_out=ssy[:, n // 2, m, n % 2:n % 2 + 1]).then_inc(y_sq, 1)

            def y_hi(r):
                half, hg, m = r
                dst = (ymT_hi, xT_hi)[half]
                act.wait_ge(yg_done, Y_NO[r] + 1)
                nc.scalar.activation(dst[:, hg * HPC:(hg + 1) * HPC, m * P:(m + 1) * P],
                                     pT[:, Y_NO[r] % 2, :].rearrange("p (h t) -> p h t", h=HPC), ACT.Copy).then_inc(yhi_done, 1)

            def final_squares(c):
                for m in range(MT):
                    act.wait_ge(dve_read, dve_reads(NC + c - 1) + m + 1)
                    act.wait_ge(*((fin_sq, 2 * c + m) if c + m else (y_sq, 8)))
                    nc.scalar.activation(junk[:, 0:CW], acc[:, m, c * CW:(c + 1) * CW], ACT.Square,
                                         accum_out=ssf[:, m, c:c + 1]).then_inc(fin_sq, 1)

            for r0, src in ((0, g_norm[0].rearrange("(k p) -> k p", p=P)), (16, g_out_moba[0].rearrange("(k p) -> k p", p=P)),
                            (24, g_out_nsa[0].rearrange("(k p) -> k p", p=P)), (32, pe_ck[0]), (64, pe_cv[0])):
                act.dma_start(crows[r0:r0 + src.shape[0], :], src).then_inc(crow_in, 16)
            with nc.allow_non_contiguous_dma(reason="256 positions"):
                act.dma_start(pos_i[:, :], positions[0].rearrange("(m p) -> p m", p=P)).then_inc(trig_in, 16)
            act.dma_start(invf[:, :], inv_freq).then_inc(trig_in, 16)
            with nc.allow_non_contiguous_dma(reason="24 gate columns"):
                act.dma_start(wg[:, :, :], w_in[0, :, COL_G:COL_G + NGATE].rearrange("(k p) c -> p k c", p=P)).then_inc(wg_in, 16)
            for n, w in enumerate((w_ck2, w_cv2)):
                act.dma_start(w2[:, n, :, :], w[0].rearrange("(t p) d -> p t d", p=P)).then_inc(w2_in, 16)
            x_hi(0)
            x_hi(1)
            hi(0)
            x_hi(2)
            x_hi(3)
            hi(1)
            for slot in range(NSLOT):
                if slot + 2 < NSLOT:
                    hi(slot + 2)
                if slot < 2:
                    x_hi(4 + 2 * slot)
                    x_hi(5 + 2 * slot)
                if slot == 1:
                    for q in range(4):
                        act.wait_ge(x_in[q], 16)
                    for m in range(MT):
                        if m:
                            act.wait_ge(sq_done, m)
                        nc.scalar.activation(junk, xo[:, m, :], ACT.Square, accum_out=ssx[:, m:m + 1]).then_inc(sq_done, 1)
                if slot == 3:
                    act.wait_ge(trig_arg, 2)
                    nc.scalar.activation(trig[:, 2, :], trig[:, 2, :], ACT.Sin).then_inc(trig_act, 1)
                    nc.scalar.activation(trig[:, 3, :], trig[:, 3, :], ACT.Sin).then_inc(trig_act, 1)
                if slot in ROUNDS:
                    round_out(slot)
                if slot - 1 in JOB_AT:
                    exps(JOB_AT[slot - 1])
                if slot - 2 in JOB_AT:
                    prob_out(JOB_AT[slot - 2])
                if slot % UPC == UPC - 1 and slot < NPROJ and ACT_READS[KINDS[slot // UPC]]:
                    evac(slot // UPC)
                if slot in (CK_SLOT[3], CK_SLOT[7]):
                    hidden_exp((CK_SLOT[3], CK_SLOT[7]).index(slot))
                if slot in CK2_SLOT:
                    ck2_evac(CK2_SLOT.index(slot))
                if slot == GATE_SLOT - 2:
                    act.wait_ge(wg_in, 16)
                    nc.scalar.activation(wg_hi[:, :, :], wg[:, :, :], ACT.Copy).then_inc(wghi_ok, 1)
                if slot == GATE_SLOT:
                    act.wait_ge(gates_done, 1)
                    for m in range(MT):
                        nc.scalar.activation(gate[:, m, :], b_o[:, 384 + m * NGATE:384 + (m + 1) * NGATE], ACT.Exp,
                                             scale=nrstd[:, m:m + 1]).then_inc(gate_exp, 1)
                if slot in (49, 52, 56, 60):
                    y_squares((49, 52, 56, 60).index(slot))
                for r in Y_ROUNDS.get(slot, []):
                    y_hi(r)
                if slot in OUT_DONE:
                    final_squares(OUT_DONE.index(slot))
            act.wait_ge(rstdf_ok, 1)
            act.wait_ge(fin_dve, 1)
            nc.scalar.activation(acc[:, 1, :], acc[:, 1, :], ACT.Copy, scale=rstdf[:, 1:2]).then_inc(fin_act, 1)

        @block.vector
        def _(dve):
            steps = [0]

            def link(ins):
                steps[0] += 1
                ins.then_inc(dve_step, 1)
                dve.wait_ge(dve_step, steps[0])

            def lo(u):
                dve.wait_ge(hi_ready, u + 1)
                nc.vector.tensor_tensor(w_lo[:, u % SPL], w_raw[:, u % RAW], w_hi[:, u % SPL].bitcast(F32),
                                        ALU.subtract).then_inc(lo_ready, 1)

            def x_g(r):
                q, m = r // 2, r % 2
                dve.wait_ge(x_round, r + 1)
                if r >= 2:
                    dve.wait_ge(xlo_done, r - 1)
                g = ccols[:, q * UK:(q + 1) * UK].unsqueeze(2).to_broadcast([P, UK, P])
                nc.vector.tensor_tensor(rope_a[:, r % 2, :].rearrange("p (k t) -> p k t", k=UK),
                                        xbanks[r % 4][:, :].rearrange("p (k t) -> p k t", k=UK), g, ALU.mult).then_inc(xg_done, 1)

            def angles():
                dve.wait_ge(trig_in, 32)
                link(nc.vector.tensor_copy(pos_f[:, :], pos_i[:, :]))
                ang, n, r, c = (trig[:, i, :] for i in range(4))
                for m in range(MT):
                    link(nc.vector.tensor_scalar(trig[:, 0, m * HALF:(m + 1) * HALF], invf[:, :], pos_f[:, m:m + 1], None, ALU.mult))
                link(nc.vector.tensor_scalar(n, ang, INV_2PI, MAGIC, ALU.mult, ALU.add))
                link(nc.vector.tensor_scalar(n, n, MAGIC, None, ALU.subtract))
                link(nc.vector.scalar_tensor_tensor(r, n, -C1, ang, ALU.mult, ALU.add))
                link(nc.vector.scalar_tensor_tensor(r, n, -C2, r, ALU.mult, ALU.add))
                link(nc.vector.scalar_tensor_tensor(r, n, -C3, r, ALU.mult, ALU.add))
                link(nc.vector.tensor_scalar(r, r, PI, -PI, ALU.min, ALU.max))
                link(nc.vector.scalar_tensor_tensor(c, r, -1.0, r, ALU.mult, ALU.max))
                nc.vector.tensor_scalar(c, c, -1.0, 1.5707963267948966, ALU.mult, ALU.add).then_inc(trig_arg, 2)

            def tables():
                dve.wait_ge(trig_act, 2)
                dve.wait_ge(rstd_ok, 1)
                for m in range(MT):
                    sn, cs = trig[:, 2, m * HALF:(m + 1) * HALF], trig[:, 3, m * HALF:(m + 1) * HALF]
                    nc.vector.tensor_scalar(rope_c[:, m, 0:HALF], cs, rstd[:, m:m + 1], None, ALU.mult).then_inc(tables_ok, 1)
                    nc.vector.tensor_scalar(rope_c[:, m, HALF:HD], cs, rstd[:, m:m + 1], None, ALU.mult).then_inc(tables_ok, 1)
                    nc.vector.tensor_scalar(rope_s[:, m, 0:HALF], sn, rstd[:, m:m + 1], -1.0, ALU.mult, ALU.mult).then_inc(tables_ok, 1)
                    nc.vector.tensor_scalar(rope_s[:, m, HALF:HD], sn, rstd[:, m:m + 1], None, ALU.mult).then_inc(tables_ok, 1)

            def rope(i):
                kind = KINDS[i]
                nh = NG if kind == "kv" else HPC
                dve.wait_ge(unit_used, UPC * (i + 1))
                dve.wait_ge(t_round, rounds_by(UPC * i + UPC - 1))
                dve.wait_ge(rope_sum, rope_sums(i - 1))
                dve.wait_ge(tables_ok, 8)
                for m in range(MT):
                    b = proj_b[i % 2][m][:, 0:nh * HD]
                    heads = b.rearrange("p (h d) -> p h d", h=nh)
                    halves = b.rearrange("p (h a d) -> p h a d", h=nh, a=2)
                    cosb = rope_c[:, m, :].unsqueeze(1).to_broadcast([P, nh, HD])
                    nc.vector.tensor_tensor(rope_a[:, m, 0:nh * HD].rearrange("p (h d) -> p h d", h=nh), heads, cosb,
                                            ALU.mult).then_inc(dve_read, 1)
                    sinb = rope_s[:, m, :].rearrange("p (a d) -> p a d", a=2).unsqueeze(1).to_broadcast([P, nh, 2, HALF])
                    nc.vector.tensor_tensor(rope_b[:, m, 0:nh * HD].rearrange("p (h a d) -> p h a d", h=nh, a=2),
                                            halves[:, :, ::-1, :], sinb, ALU.mult).then_inc(dve_read, 1)

            def kc_out(slot):
                _, m, _ = ROUNDS[slot]
                dve.wait_ge(t_round, ROUND_NO[slot] + 1)
                for kv in range(2):
                    src = b_t[:, kv * 2 * P:(kv + 1) * 2 * P].rearrange("p (a l) -> p a l", l=CS)
                    for half in range(2):
                        pe_ = ccols[:, 32 + kv * CL + half * CS:32 + kv * CL + (half + 1) * CS].unsqueeze(1).unsqueeze(1)
                        dst = kvpe[:, kv, half, :, m * P:(m + 1) * P].rearrange("p g (n l) -> p g n l", l=CS)
                        last = nc.vector.tensor_tensor(dst, src.rearrange("p (g n) l -> p g n l", g=NG),
                                                       pe_.to_broadcast([P, NG, P // CS, CS]), ALU.add)
                last.then_inc(t_out, 1)

            def hidden(kv):
                dve.wait_ge(ck_exp, kv + 1)
                w = 2 * NCMP
                link(nc.vector.tensor_scalar(hid_e[:, :, 0:w], hid_e[:, :, 0:w], 1.0, None, ALU.add))
                link(nc.vector.reciprocal(hid_e[:, :, 0:w], hid_e[:, :, 0:w]))
                for ht in range(2):
                    last = nc.vector.tensor_tensor(hidT[:, kv, ht, 0:w], (b_s, b_p)[ht][:, kv * 32:kv * 32 + w],
                                                   hid_e[:, ht, 0:w], ALU.mult)
                last.then_inc(hid_ready, 1)

            def gates():
                dve.wait_ge(gate_exp, 2)
                link(nc.vector.tensor_scalar(gate[:, :, :], gate[:, :, :], 1.0, None, ALU.add))
                link(nc.vector.reciprocal(gate[:, :, :], gate[:, :, :]))
                v = gate[:, :, :].rearrange("p m (h b) -> p m h b", b=3)
                for b in range(2):
                    for n, (m, br) in enumerate(((0, 1 + b), (1, 1 + b), (b, 0))):
                        last = nc.vector.tensor_copy(gate_j[:, :, b, n], v[:, m, :, br])
                last.then_inc(gates_ok, 1)

            def row_max(j):
                kind, b = JOBS[j][1], JOBS[j][3]
                dve.wait_ge(scores_done, j + 1)
                if j == 0:
                    dve.wait_ge(consts_ok, 4)
                pieces = [(0, P, 0), (P, 3 * P, P)] + ([(3 * P, 3 * P + NCMP, 3 * P + 16 * b)] if kind == "nsa" else [])
                for n, (c0, c1, k0) in enumerate(pieces):
                    nc.vector.tensor_tensor_reduce(out=prob[:, j % 2, c0:c1], in0=b_s[:, c0:c1], in1=mask[:, k0:k0 + c1 - c0],
                                                   scale=1.0, scalar=NEG, op0=ALU.add, op1=ALU.max,
                                                   accum_out=mx[:, j % 2, n:n + 1]).then_inc(s_read, 1)
                dve.wait_ge(s_read, score_reads(j))
                nc.vector.tensor_scalar(nmx[:, j % 2, 0:len(pieces)], mx[:, j % 2, 0:len(pieces)], FLOOR, -SCALE,
                                        ALU.max, ALU.mult).then_inc(negmax_ok, 1)

            def normalise(j):
                _, kind, h, b = JOBS[j]
                n = 3 if kind == "nsa" else 2
                c = coef[:, j % 2, 0:n]
                dve.wait_ge(exp_done, j + 1)
                link(nc.vector.tensor_scalar(c, sums[:, j % 2, 0:n], 1e-30, None, ALU.max))
                link(nc.vector.reciprocal(c, c))
                if kind == "nsa":
                    link(nc.vector.tensor_tensor(c, c, gate_j[:, h, b, 0:3], ALU.mult))
                for i, (c0, c1) in enumerate(((0, P), (P, 3 * P), (3 * P, 3 * P + NCMP))[:n]):
                    last = nc.vector.tensor_scalar(prob[:, j % 2, c0:c1], prob[:, j % 2, c0:c1], coef[:, j % 2, i:i + 1], None, ALU.mult)
                last.then_inc(prob_ready, 1)

            def o_evac(j):
                _, kind, h, _ = JOBS[j]
                col = (0 if kind == "moba" else HW) + h * HD
                dve.wait_ge(pv_done, heads_done(j))
                nc.vector.tensor_copy(xo[:, :, col:col + HD], b_o[:, 0:2 * P].rearrange("p (m d) -> p m d", m=MT)).then_inc(o_out, 1)

            def silu(i):
                n = CHUNKS[i][2]
                z = (rope_a, rope_b)[n % 2]
                for m in range(MT):
                    dve.wait_ge(act_read, act_reads(i - 1) + m + 1)
                    nc.vector.scalar_tensor_tensor(z[:, m, :], proj_b[i % 2][m][:, :], rstd[:, m:m + 1], z[:, m, :],
                                                   ALU.mult, ALU.mult).then_inc(dve_read, 1)

            def y_scale(half):
                dve.wait_ge(rstdy_ok, half + 1)
                for m in range(MT):
                    y = xo[:, m, half * HW:(half + 1) * HW]
                    nc.vector.tensor_scalar(y, y, rstdy[:, half, m:m + 1], None, ALU.mult).then_inc(y_scaled, 1)

            def y_parts(r):
                half, hg, m = r
                n = Y_NO[r]
                bank_ = b_t if half == 0 else (b_t, b_s, b_p, b_o)[n - 4]
                dve.wait_ge(y_round, n + 1)
                dve.wait_ge(pt_out, len(JOBS))
                g0 = 16 + half * NH + hg * HPC
                yg = pT[:, n % 2, :].rearrange("p (h t) -> p h t", h=HPC)
                nc.vector.tensor_tensor(yg, bank_[:, :].rearrange("p (h t) -> p h t", h=HPC),
                                        ccols[:, g0:g0 + HPC].unsqueeze(2).to_broadcast([P, HPC, P]), ALU.mult).then_inc(yg_done, 1)
                dve.wait_ge(yhi_done, n + 1)
                hi_, lo_ = ((ymT_hi, ymT_lo), (xT_hi, xT_lo))[half]
                sl = (slice(None), slice(hg * HPC, (hg + 1) * HPC), slice(m * P, (m + 1) * P))
                nc.vector.tensor_tensor(lo_[sl], yg, hi_[sl].bitcast(F32), ALU.subtract).then_inc(ylo_done, 1)

            def residual(c):
                dve.wait_ge(unit_used, OUT_DONE[c] + 1)
                if c == 0:
                    dve.wait_ge(acc_in, 16)
                for m in range(MT):
                    a = acc[:, m, c * CW:(c + 1) * CW]
                    nc.vector.tensor_tensor(a, proj_b[(NC + c) % 2][m][:, :], a, ALU.add).then_inc(dve_read, 1)

            dve.wait_ge(crows_T, 1)
            nc.vector.tensor_copy(ccols[:, :], b_p[:, 0:96]).then_inc(cols_ok, 1)
            dve.wait_ge(cols_ok, 1)
            x_g(0)
            x_g(1)
            lo(0)
            x_g(2)
            x_g(3)
            lo(1)
            for slot in range(NSLOT):
                if slot + 2 < NSLOT:
                    lo(slot + 2)
                if slot < 2:
                    x_g(4 + 2 * slot)
                    x_g(5 + 2 * slot)
                if slot == 2:
                    angles()
                if slot == 4:
                    tables()
                if slot in ROUNDS and ROUNDS[slot][0] == "kc":
                    kc_out(slot)
                if slot - 1 in JOB_AT:
                    normalise(JOB_AT[slot - 1])
                if slot - 3 in JOB_AT and ends_head(JOB_AT[slot - 3]):
                    o_evac(JOB_AT[slot - 3])
                if slot in JOB_AT:
                    row_max(JOB_AT[slot])
                if slot % UPC == UPC - 1 and slot < NPROJ:
                    if KINDS[slot // UPC] in ROPED:
                        rope(slot // UPC)
                    if KINDS[slot // UPC] == "z":
                        silu(slot // UPC)
                if slot in (CK_SLOT[3], CK_SLOT[7]):
                    hidden((CK_SLOT[3], CK_SLOT[7]).index(slot))
                if slot == GATE_SLOT - 2:
                    dve.wait_ge(wghi_ok, 1)
                    nc.vector.tensor_tensor(wg_lo[:, :, :], wg[:, :, :], wg_hi[:, :, :].bitcast(F32), ALU.subtract).then_inc(wglo_ok, 1)
                if slot == GATE_SLOT:
                    gates()
                if slot in (53, 61):
                    y_scale((53, 61).index(slot))
                for r in Y_ROUNDS.get(slot, []):
                    y_parts(r)
                if slot in OUT_DONE:
                    residual(OUT_DONE.index(slot))
            dve.wait_ge(fin_sq, 8)
            nc.vector.tensor_reduce(ssf1[:, :], ssf[:, :, :], mybir.AxisListType.X, ALU.add).then_inc(ssf_ok, 1)
            dve.wait_ge(gfin_in, 16)
            for m in range(MT):
                a = acc[:, m, 3 * CW:4 * CW]
                link(nc.vector.tensor_tensor(a, a, g_fin[:, 3 * CW:4 * CW], ALU.mult))
            dve.wait_ge(rstdf_ok, 1)
            dve.wait_ge(gmul, 6)
            nc.vector.tensor_scalar(acc[:, 0, :], acc[:, 0, :], rstdf[:, 0:1], None, ALU.mult).then_inc(fin_dve, 1)


_INS = ["x", "positions", "inv_freq", "w_in", "g_norm", "pe_ck", "pe_cv", "w_ck1", "w_ck2", "w_cv1", "w_cv2",
        "g_out_moba", "g_out_nsa", "w_out", "g_final"]


def kernel(**inputs):
    import numpy as _np
    import concourse.bacc as _bacc
    from concourse import mybir as _mybir
    from concourse.bass_utils import run_bass_kernel_spmd as _run

    freq = 1.0 / (_np.float32(10000.0) ** (_np.arange(0, HD, 2, dtype=_np.float32) / _np.float32(HD)))
    inv_freq = _np.ascontiguousarray(_np.broadcast_to(freq.astype(_np.float32), (P, HALF)))
    nc = _bacc.Bacc("TRN2", target_bir_lowering=False, num_devices=1)
    arrays, args = {}, []
    for name in _INS:
        a = inv_freq if name == "inv_freq" else _np.ascontiguousarray(inputs[name])
        arrays[f"in_{name}_dram"] = a
        args.append(nc.dram_tensor(f"in_{name}_dram", a.shape, _mybir.dt.from_np(a.dtype), kind="ExternalInput").ap())
    args.append(nc.dram_tensor("out_dram", (1, S, D), _mybir.dt.float32, kind="ExternalOutput").ap())
    build_layer(nc, *args)
    r = _run(nc, [arrays], core_ids=[0])
    return r.results[0]["out_dram"]
```

```python
import concourse.bass as bass
from concourse import mybir
from contextlib import ExitStack


S, D, P, HD = 256, 2048, 128, 128
MT = S // P
KT = D // P
NH = 8
HW = NH * HD
CW = 512
UK = 4
UPC = KT // UK
HPC = CW // HD
NG, NGATE = 2, 24
NCMP, CL, CS, CH = 15, 32, 16, 256
SCALE = HD ** -0.5
EPS = 1e-6
NEG = -3.0e38
FLOOR = -1.0e38
HALF = HD // 2

COL_MQ, COL_MK, COL_MV, COL_MZ = 0, HW, 2 * HW, 3 * HW
COL_NQ = 4 * HW
COL_KC = 5 * HW
COL_KS, COL_KW, COL_G = COL_KC + 512, COL_KC + 1024, COL_KC + 1536
COL_NZ = COL_G + NGATE
CHUNKS = [("kc", COL_KC, 0), ("kv", COL_KS, 0), ("kv", COL_KW, 1), ("nq", COL_NQ, 0), ("nq", COL_NQ + CW, 1),
          ("mq", COL_MQ, 0), ("mk", COL_MK, 0), ("mv", COL_MV, 0), ("mq", COL_MQ + CW, 1),
          ("mk", COL_MK + CW, 1), ("mv", COL_MV + CW, 1),
          ("z", COL_MZ, 0), ("z", COL_MZ + CW, 1), ("z", COL_NZ, 2), ("z", COL_NZ + CW, 3)]
NC = len(CHUNKS)
NPROJ = NC * UPC
OUT_UNITS = [(0, 0), (0, 1), (1, 0), (1, 1), (0, 2), (1, 2), (0, 3), (1, 3)] + [(c, g) for c in (2, 3) for g in range(4)]
NSLOT = NPROJ + len(OUT_UNITS)
OUT_DONE = [NPROJ + max(i for i, u in enumerate(OUT_UNITS) if u[0] == c) for c in range(4)]
RAW, SPL = 3, 3

ACT_READS = {"kc": 2, "kv": 2, "nq": 2, "mq": 0, "mk": 0, "mv": 2, "z": 2, "out": 0}
DVE_READS = {"kc": 0, "kv": 4, "nq": 4, "mq": 4, "mk": 4, "mv": 0, "z": 2, "out": 2}
KINDS = [c[0] for c in CHUNKS] + ["out"] * 4
ROPED = ("kv", "nq", "mq", "mk")


def act_reads(i):
    return sum(ACT_READS[k] for k in KINDS[:i + 1])


def dve_reads(i):
    return sum(DVE_READS[k] for k in KINDS[:i + 1])


def rope_sums(i):
    return 2 * sum(k in ROPED for k in KINDS[:i + 1])


Q_ROT, Q_RAW, Q_KS, Q_MQ, Q_MK = 0, 8, 16, [20, 0], [24, 8]


def transpose_rounds():
    out = {}
    for i, (kind, _, n) in enumerate(CHUNKS):
        s = UPC * i + UPC
        if kind == "kc":
            out[s], out[s + 1] = ("kc", 0, i), ("kc", 1, i)
        elif kind == "kv":
            out[s] = ("kv", n, i)
        elif kind == "nq":
            for k, m in ((0, 0), (0, 1), (1, 0), (1, 1)):
                out[s + 2 * k + m] = (("rot", "raw")[k], (n, m), i)
        elif kind in ("mq", "mk"):
            out[s], out[s + 1] = (kind, (n, 0), i), (kind, (n, 1), i)
    return out


ROUNDS = transpose_rounds()
ROUND_NO = {s: n for n, s in enumerate(sorted(ROUNDS))}


def rounds_by(slot):
    return sum(s <= slot for s in ROUNDS)


JOBS = [(20 + 2 * h + b, "nsa", h, b) for h in range(8) for b in range(2)] + \
       [(36 + h, "moba", h, 0) for h in range(4)] + [(42 + h, "moba", 4 + h, 0) for h in range(4)]
JOB_AT = {j[0]: n for n, j in enumerate(JOBS)}
LAST_JOB_SLOT = JOBS[-1][0]


def score_reads(j):
    return sum(3 if JOBS[i][1] == "nsa" else 2 for i in range(j + 1))


def ends_head(j):
    return JOBS[j][1] == "moba" or JOBS[j][3] == 1


def heads_done(j):
    return sum(ends_head(i) for i in range(j + 1))


CK_SLOT = [6, 7, 9, 10, 12, 13, 15, 16]
CK_AT = {s: c for c, s in enumerate(CK_SLOT)}
CK_SUM_SLOT = [11, 17]
CK2_SLOT = [12, 18]
GATE_SLOT = 13
TP = 2 * CS
Y_ROUNDS = {54: [(0, 0, 0)], 55: [(0, 0, 1)], 56: [(0, 1, 0)], 57: [(0, 1, 1)],
            62: [(1, 0, 0), (1, 0, 1)], 63: [(1, 1, 0), (1, 1, 1)]}
Y_NO = {r: n for n, r in enumerate(r for s in sorted(Y_ROUNDS) for r in Y_ROUNDS[s])}

INV_2PI = 0.15915494309189535
MAGIC = 12582912.0
C1 = 6.28125
C2 = 0.0019350051879882812
C3 = 6.283185307179586 - C1 - C2
PI = 3.1415925


def build_layer(nc, x, positions, inv_freq, w_in, g_norm, pe_ck, pe_cv, w_ck1, w_ck2, w_cv1, w_cv2,
                g_out_moba, g_out_nsa, w_out, g_final, out):
    F32, F32R, BF16, I32 = mybir.dt.float32, mybir.dt.float32r, mybir.dt.bfloat16, mybir.dt.int32
    ALU, ACT = mybir.AluOpType, mybir.ActivationFunctionType

    with ExitStack() as ctx:
        def sb(name, shape, dt=F32):
            return ctx.enter_context(nc.sbuf_tensor(name, shape, dt))

        def sem(name):
            return ctx.enter_context(nc.semaphore(name))

        xo = sb("xo", [P, MT, D])
        xT_hi, xT_lo = sb("xT_hi", [P, KT, S], F32R), sb("xT_lo", [P, KT, S], F32R)
        ymT_hi, ymT_lo = sb("ymT_hi", [P, NH, S], F32R), sb("ymT_lo", [P, NH, S], F32R)
        w_raw = sb("w_raw", [P, RAW, UK, CW])
        w_hi, w_lo = sb("w_hi", [P, SPL, UK, CW], F32R), sb("w_lo", [P, SPL, UK, CW], F32R)
        Q = sb("Q", [P, 28, S])
        acc = Q[:, 0:16, :].rearrange("p a b -> p (a b)").rearrange("p (m d) -> p m d", m=MT)
        g_fin = Q[:, 16:24, :].rearrange("p a b -> p (a b)")
        KV8 = sb("KV8", [P, D + CS])
        kvpe = KV8[:, 0:D].rearrange("p (v h g t) -> p v h g t", v=2, h=2, g=NG)
        mv = KV8[:, 0:D].rearrange("p (m c) -> p m c", m=MT)
        nv = sb("nv", [P, 2, MT, 2 * HD])
        rope_a, rope_b = sb("rope_a", [P, MT, CW]), sb("rope_b", [P, MT, CW])
        raw_e = sb("raw_e", [P, MT, CW])
        junk = raw_e[:, :, :].rearrange("p m c -> p (m c)").bitcast(BF16)
        prob = sb("prob", [P, 2, 400])
        w2 = prob[:, :, :].rearrange("p a b -> p (a b)")[:, 0:4 * HD].rearrange("p (v t d) -> p v t d", v=2, t=2)
        pT = sb("pT", [P, 2, 512])
        trig = pT[:, 0, :].rearrange("p (a c) -> p a c", a=4)
        crows, grows = pT[0:80, 1, 0:P], pT[0:16, 1, P:2 * P]
        quarters = pT[:, 1, 0:CH]
        ident = sb("ident", [P, P])
        mask = sb("mask", [P, 3 * P + 2 * NCMP + 2])
        ccols = sb("ccols", [P, 96])
        invf, pos_i, pos_f = sb("invf", [P, HALF]), sb("pos_i", [P, MT], I32), sb("pos_f", [P, MT])
        rope_c, rope_s = sb("rope_c", [P, MT, HD]), sb("rope_s", [P, MT, HD])
        ssx, rstd, nrstd = sb("ssx", [P, MT]), sb("rstd", [P, MT]), sb("nrstd", [P, MT])
        half_c = sb("half_c", [P, MT])
        mx, sums, coef = sb("mx", [P, 2, 4]), sb("sums", [P, 2, 4]), sb("coef", [P, 2, 4])
        nmx = sb("nmx", [P, 2, 4])
        wg = sb("wg", [P, KT, 32])
        sel = sb("sel", [P, 32])
        gate, gate_j = sb("gate", [P, MT, NGATE]), sb("gate_j", [P, NH, 2, 4])
        hid_e, hidT = sb("hid_e", [P, 2, TP]), sb("hidT", [P, 2, 2, TP])
        kcT, vc = sb("kcT", [P, TP]), sb("vc", [16, NG, HD])
        ssy, rstdy = sb("ssy", [P, 2, MT, 2]), sb("rstdy", [P, 2, MT])
        ssf, ssf1, rstdf = sb("ssf", [P, MT, 4]), sb("ssf1", [P, MT]), sb("rstdf", [P, MT])

        def bank(name):
            return ctx.enter_context(nc.psum_tensor(name, [P, 512], F32))

        proj_b = [[bank(f"proj{i}{m}") for m in range(MT)] for i in range(2)]
        b_s, b_o, b_t, b_p = bank("b_s"), bank("b_o"), bank("b_t"), bank("b_p")
        xbanks = [b_s, b_o, b_t, b_p]

        x_in = [sem(f"x_in{q}") for q in range(5)]
        w0_in = [sem(f"w0_in{k}") for k in range(UK)]
        raw_in = [sem(f"raw_in{i}") for i in range(RAW)]
        ck_in = [sem(f"ck_in{i}") for i in range(2)]
        grow_in, crow_in, trig_in, wg_in, w2_in = sem("grow_in"), sem("crow_in"), sem("trig_in"), sem("wg_in"), sem("w2_in")
        acc_in, gfin_in, out_in = sem("acc_in"), sem("gfin_in"), sem("out_in")
        ident_ok, consts_ok, pool_step = sem("ident_ok"), sem("consts_ok"), sem("pool_step")
        sel_ok, xlo_even, rstd_ok, rope_sum, y_done = sem("sel_ok"), sem("xlo_even"), sem("rstd_ok"), sem("rope_sum"), sem("y_done")
        rstdy_ok, rstdf_ok = sem("rstdy_ok"), sem("rstdf_ok")
        gmul = sem("gmul")
        crows_T, x_round, unit_used, t_round = sem("crows_T"), sem("x_round"), sem("unit_used"), sem("t_round")
        ck_used, ck_sum, ck2_done = sem("ck_used"), sem("ck_sum"), sem("ck2_done")
        gates_done, gates_sum, m0_done = sem("gates_done"), sem("gates_sum"), sem("m0_done")
        scores_done, pt_done, pv_done, y_round = sem("scores_done"), sem("pt_done"), sem("pv_done"), sem("y_round")
        hi_ready, xhi_done, sq_done, trig_act = sem("hi_ready"), sem("xhi_done"), sem("sq_done"), sem("trig_act")
        act_read, ck_exp, ck2_out, gate_exp = sem("act_read"), sem("ck_exp"), sem("ck2_out"), sem("gate_exp")
        w0_hi, quarters_ok, exp_done, pt_out, y_sq = sem("w0_hi"), sem("quarters_ok"), sem("exp_done"), sem("pt_out"), sem("y_sq")
        yhi_done, fin_sq, fin_act = sem("yhi_done"), sem("fin_sq"), sem("fin_act")
        cols_ok, xg_done, lo_ready, dve_read = sem("cols_ok"), sem("xg_done"), sem("lo_ready"), sem("dve_read")
        dve_step, trig_arg, tables_ok = sem("dve_step"), sem("trig_arg"), sem("tables_ok")
        hid_ready, w0_lo, gates_ok, xlo_odd = sem("hid_ready"), sem("w0_lo"), sem("gates_ok"), sem("xlo_odd")
        s_read, negmax_ok, prob_ready, o_out = sem("s_read"), sem("negmax_ok"), sem("prob_ready"), sem("o_out")
        y_scaled, yg_done, ylo_done, ssf_ok, fin_dve = sem("y_scaled"), sem("yg_done"), sem("ylo_done"), sem("ssf_ok"), sem("fin_dve")
        t_out = sem("t_out")

        block = ctx.enter_context(nc.Block())

        def unit_src(u):
            if u < NPROJ:
                col, g = CHUNKS[u // UPC][1], u % UPC
                src = w_in[0, g * UK * P:(g + 1) * UK * P, col:col + CW]
            else:
                c, g = OUT_UNITS[u - NPROJ]
                src = w_out[0, g * UK * P:(g + 1) * UK * P, c * CW:(c + 1) * CW]
            return src.rearrange("(k p) c -> p k c", p=P)

        @block.sync
        def _(sp):
            def x_quarter(q):
                if q == 0:
                    for m in range(MT):
                        sp.dma_start(xo[:, m, 0:CW], x[0, m * P:(m + 1) * P, 0:CW]).then_inc(x_in[4 * m], 16)
                else:
                    sp.dma_start(xo[:, :, q * CW:(q + 1) * CW],
                                 x[0, :, q * CW:(q + 1) * CW].rearrange("(m p) c -> p m c", p=P)).then_inc(x_in[q], 16)

            def unit(u):
                if u == RAW:
                    sp.wait_ge(w0_lo, UK)
                if u > RAW:
                    sp.wait_ge(lo_ready, u - RAW)
                sp.dma_start(w_raw[:, u % RAW], unit_src(u)).then_inc(raw_in[u % RAW], 16)

            def ck_unit(c):
                if c == 0:
                    sp.wait_ge(sq_done, 2)
                    sp.wait_ge(x_round, 8)
                if c >= 2:
                    sp.wait_ge(ck_used, c - 1)
                w = (w_ck1, w_cv1)[c // 4]
                l0 = (c % 4) * 8
                sp.dma_start(xo[:, c % 2, :].rearrange("p (l h) -> p l h", l=8),
                             w[0, l0 * HD:(l0 + 8) * HD, :].rearrange("(l d) h -> d l h", d=HD)).then_inc(ck_in[c % 2], 16)

            x_quarter(0)
            for k in range(UK):
                sp.dma_start(w_raw[:, 0, k, :], w_in[0, k * P:(k + 1) * P, CHUNKS[0][1]:CHUNKS[0][1] + CW]).then_inc(w0_in[k], 16)
            x_quarter(1)
            unit(1)
            x_quarter(2)
            unit(2)
            x_quarter(3)
            ck_next = 0
            for u in range(RAW, NSLOT):
                unit(u)
                while ck_next < 8 and u >= CK_SLOT[ck_next] and u >= 6:
                    ck_unit(ck_next)
                    ck_next += 1
                if u == 54:
                    sp.wait_ge(scores_done, len(JOBS))
                    sp.dma_start(acc, x[0].rearrange("(m p) c -> p m c", p=P)).then_inc(acc_in, 16)
                if u == 56:
                    sp.dma_start(g_fin, g_final.rearrange("(a d) -> a d", a=1).to_broadcast([P, D])).then_inc(gfin_in, 16)
            for m in range(MT):
                for h, done in enumerate((fin_act, fin_dve)):
                    sp.wait_ge(done, m + 1)
                    sp.dma_start(out[0, m * P:(m + 1) * P, h * HW:(h + 1) * HW], acc[:, m, h * HW:(h + 1) * HW]).then_inc(out_in, 16)
            sp.wait_ge(out_in, 32 * MT)

        @block.gpsimd
        def _(pool):
            steps = [0]

            def link(ins):
                steps[0] += 1
                ins.then_inc(pool_step, 1)
                pool.wait_ge(pool_step, steps[0])

            link(nc.gpsimd.memset(ident[:, :], 0.0))
            nc.gpsimd.affine_select(out=ident[:, :], in_=ident[:, :], compare_op=ALU.not_equal, fill=1.0, base=0,
                                    pattern=[[-1, P]], channel_multiplier=1).then_inc(ident_ok, 1)
            nc.gpsimd.memset(half_c[:, :], -0.5)
            link(nc.gpsimd.memset(mask[:, :], 0.0))
            for c0, n, step, base in ((0, P, -1, 0), (2 * P, P, -1, 0), (3 * P, NCMP, -CS, 1 - CL), (3 * P + 16, NCMP, -CS, P + 1 - CL)):
                nc.gpsimd.affine_select(out=mask[:, c0:c0 + n], in_=mask[:, c0:c0 + n], compare_op=ALU.is_ge, fill=NEG,
                                        base=base, pattern=[[step, n]], channel_multiplier=1).then_inc(consts_ok, 1)
            link(nc.gpsimd.memset(sel[:, :], 0.0))
            for n in range(4):
                link(nc.gpsimd.affine_select(out=sel[:, :], in_=sel[:, :], compare_op=ALU.not_equal, fill=1.0, base=-32 * n,
                                             pattern=[[-1, 32]], channel_multiplier=1))
            nc.gpsimd.memset(KV8[:, D:], 0.0).then_inc(sel_ok, 1)
            for r in range(0, 8, 2):
                q, m = r // 2, r % 2
                pool.wait_ge(xhi_done, r + 1)
                nc.gpsimd.tensor_tensor(xT_lo[:, q * UK:(q + 1) * UK, m * P:(m + 1) * P],
                                        rope_a[:, r % 2, :].rearrange("p (k t) -> p k t", k=UK),
                                        xT_hi[:, q * UK:(q + 1) * UK, m * P:(m + 1) * P].bitcast(F32),
                                        ALU.subtract).then_inc(xlo_even, 1)
            pool.wait_ge(sq_done, 2)
            link(nc.gpsimd.tensor_scalar(ssx[:, :], ssx[:, :], 1.0 / D, EPS, ALU.mult, ALU.add))
            nc.gpsimd.tensor_tensor(rstd[:, :], ssx[:, :], half_c[:, :], ALU.pow).then_inc(rstd_ok, 1)
            pool.wait_ge(rstd_ok, 1)
            nc.gpsimd.tensor_scalar(nrstd[:, :], rstd[:, :], -1.0, None, ALU.mult).then_inc(rstd_ok, 1)
            for i, kind in enumerate(KINDS[:NC]):
                if kind in ROPED:
                    w = 2 * HD if kind == "kv" else CW
                    for m in range(MT):
                        pool.wait_ge(dve_read, dve_reads(i - 1) + 2 * (m + 1))
                        nc.gpsimd.tensor_tensor(rope_a[:, m, 0:w], rope_a[:, m, 0:w], rope_b[:, m, 0:w],
                                                ALU.add).then_inc(rope_sum, 1)
                elif kind == "z":
                    n = CHUNKS[i][2]
                    z = (rope_a, rope_b)[n % 2]
                    if n == 0:
                        pool.wait_ge(o_out, 2 * NH)
                    for m in range(MT):
                        pool.wait_ge(dve_read, dve_reads(i - 1) + m + 1)
                        nc.gpsimd.tensor_tensor(xo[:, m, n * CW:(n + 1) * CW], xo[:, m, n * CW:(n + 1) * CW],
                                                z[:, m, :], ALU.mult).then_inc(y_done, 1)
                    if n % 2:
                        h = n // 2
                        pool.wait_ge(y_sq, 4 * (h + 1))
                        link(nc.gpsimd.tensor_tensor(rstdy[:, h, :], ssy[:, h, :, 0], ssy[:, h, :, 1], ALU.add))
                        link(nc.gpsimd.tensor_scalar(rstdy[:, h, :], rstdy[:, h, :], 1.0 / HW, EPS, ALU.mult, ALU.add))
                        nc.gpsimd.tensor_tensor(rstdy[:, h, :], rstdy[:, h, :], half_c[:, :], ALU.pow).then_inc(rstdy_ok, 1)
            pool.wait_ge(gfin_in, 16)
            for c in range(3):
                for m in range(MT):
                    pool.wait_ge(fin_sq, 2 * c + m + 1)
                    nc.gpsimd.tensor_tensor(acc[:, m, c * CW:(c + 1) * CW], acc[:, m, c * CW:(c + 1) * CW],
                                            g_fin[:, c * CW:(c + 1) * CW], ALU.mult).then_inc(gmul, 1)
            for m in range(MT):
                pool.wait_ge(ssf_ok, m + 1)
                link(nc.gpsimd.tensor_scalar(ssf1[:, m:m + 1], ssf1[:, m:m + 1], 1.0 / D, EPS, ALU.mult, ALU.add))
                nc.gpsimd.tensor_tensor(rstdf[:, m:m + 1], ssf1[:, m:m + 1], half_c[:, m:m + 1], ALU.pow).then_inc(rstdf_ok, 1)

        @block.tensor
        def _(pe):
            def transpose4(bank_, srcs, done):
                for n, src in enumerate(srcs):
                    last = nc.tensor.transpose(bank_[:, n * P:(n + 1) * P], src, ident[:, :])
                last.then_inc(done, 1)

            def x_round_(r):
                q, m = r // 2, r % 2
                pe.wait_ge(x_in[4 * m if q == 0 else q], 16)
                if r == 3:
                    pe.wait_ge(cols_ok, 1)
                if r >= 4:
                    pe.wait_ge(xg_done, r - 3)
                transpose4(xbanks[r % 4], [xo[:, m, (q * UK + k) * P:(q * UK + k + 1) * P] for k in range(UK)], x_round)

            def split_products(outs, stat_hi, stat_lo, k0, nk, mov_hi, mov_lo, first, last, by_row=False, signal_m0=False):
                order = [(m, k) for m in range(MT) for k in range(nk)]
                if by_row:
                    order = [(m, k) for k in range(nk) for m in range(MT)]
                for m, k in order:
                    tok = slice(m * P, (m + 1) * P)
                    if by_row and m == 0:
                        pe.wait_ge(w0_lo, k + 1)
                    a_hi, a_lo = stat_hi[:, k0 + k, tok], stat_lo[:, k0 + k, tok]
                    nc.tensor.matmul(outs[m], a_hi, mov_hi[:, k, :], start=first and k == 0, stop=False)
                    nc.tensor.matmul(outs[m], a_hi, mov_lo[:, k, :], start=False, stop=False)
                    ins = nc.tensor.matmul(outs[m], a_lo, mov_hi[:, k, :], start=False, stop=last and k == nk - 1)
                    if signal_m0 and m == 0 and k == nk - 1:
                        ins.then_inc(m0_done, 1)
                return ins

            def unit(u):
                if u < NPROJ:
                    c, g = u // UPC, u % UPC
                    if u < UPC:
                        pe.wait_ge(xlo_even, u + 1)
                        pe.wait_ge(xlo_odd, u + 1)
                    sh, sl, k0 = xT_hi, xT_lo, g * UK
                else:
                    oc, g = OUT_UNITS[u - NPROJ]
                    c = NC + oc
                    pe.wait_ge(ylo_done, 4 if g < 2 else 2 * g + 2)
                    sh, sl, k0 = (ymT_hi, ymT_lo, g * UK) if g < 2 else (xT_hi, xT_lo, (g - 2) * UK)
                if g == 0 and c >= 2:
                    pe.wait_ge(act_read, act_reads(c - 2))
                    pe.wait_ge(dve_read, dve_reads(c - 2))
                if u:
                    pe.wait_ge(lo_ready, u)
                split_products([proj_b[c % 2][m][:, :] for m in range(MT)], sh, sl, k0, UK,
                               w_hi[:, u % SPL], w_lo[:, u % SPL], g == 0, g == UPC - 1,
                               by_row=u == 0, signal_m0=u == NSLOT - 1).then_inc(unit_used, 1)

            def round_(slot):
                kind, which, i = ROUNDS[slot]
                no = ROUND_NO[slot]
                if no:
                    pe.wait_ge(t_out, no)
                else:
                    pe.wait_ge(cols_ok, 2)
                if kind == "kc":
                    pe.wait_ge(act_read, act_reads(i - 1) + which + 1)
                    srcs = [raw_e[:, which, h * HD:(h + 1) * HD] for h in range(HPC)]
                elif kind == "kv":
                    pe.wait_ge(rope_sum, rope_sums(i))
                    srcs = [rope_a[:, m, g * HD:(g + 1) * HD] for g in range(NG) for m in range(MT)]
                elif kind == "raw":
                    pe.wait_ge(act_read, act_reads(i))
                    srcs = [raw_e[:, which[1], h * HD:(h + 1) * HD] for h in range(HPC)]
                else:
                    pe.wait_ge(rope_sum, rope_sums(i - 1) + which[1] + 1)
                    srcs = [rope_a[:, which[1], h * HD:(h + 1) * HD] for h in range(HPC)]
                transpose4(b_t, srcs, t_round)

            def ck_unit(c):
                kv = c // 4
                if c == 0:
                    pe.wait_ge(t_out, 2)
                    pe.wait_ge(sel_ok, 1)
                pe.wait_ge(ck_in[c % 2], 16 * (c // 2 + 1))
                if c == 4:
                    pe.wait_ge(quarters_ok, 1)
                w = xo[:, c % 2, :].rearrange("p (l h) -> p l h", l=8)
                for l8 in range(8):
                    l, j = (c % 4) * 8 + l8, l8 % 4
                    t0 = (2 * kv + l // CS) * NG * S + l
                    last = nc.tensor.matmul(b_s[32 * j:32 * j + 32, kv * CH:(kv + 1) * CH],
                                            KV8[:, t0:t0 + CS * (TP - 1) + 1:CS], w[:, l8, :], start=l < 4, stop=l >= CL - 4)
                last.then_inc(ck_used, 1)

            def ck_quarters(kv):
                pe.wait_ge(quarters_ok, (1, 3)[kv])
                for ht in range(2):
                    last = nc.tensor.matmul(b_p[:, (2 * kv + ht) * TP:(2 * kv + ht + 1) * TP], quarters[:, ht * P:(ht + 1) * P],
                                            sel[:, :], start=True, stop=True)
                last.then_inc(ck_sum, 1)

            def ck_layer2(kv):
                if kv == 0:
                    pe.wait_ge(w2_in, 32)
                pe.wait_ge(hid_ready, kv + 1)
                if kv:
                    pe.wait_ge(gate_exp, 2)
                if kv == 0:
                    for ht in range(2):
                        last = nc.tensor.matmul(b_o[:, 0:TP], w2[:, 0, ht, :], hidT[:, 0, ht, :],
                                                start=ht == 0, stop=ht == 1)
                else:
                    for g in range(NG):
                        for ht in range(2):
                            last = nc.tensor.matmul(b_o[0:NCMP, (g + 1) * HD:(g + 2) * HD],
                                                    hidT[:, 1, ht, g * CS:g * CS + NCMP], w2[:, 1, ht, :],
                                                    start=ht == 0, stop=ht == 1)
                last.then_inc(ck2_done, 1)

            def gates():
                pe.wait_ge(wg_in, 16)
                pe.wait_ge(ck2_out, 1)
                for n, part in enumerate((xT_hi, xT_lo)):
                    for k in range(KT):
                        j = k % 4
                        last = nc.tensor.matmul(b_o[32 * j:32 * j + 32, 0:S], wg[:, k, :], part[:, k, :].bitcast(F32),
                                                start=n == 0 and k < 4, stop=n == 1 and k >= KT - 4)
                last.then_inc(gates_done, 1)

            def gate_quarters():
                pe.wait_ge(quarters_ok, 2)
                for m in range(MT):
                    last = nc.tensor.matmul(b_o[:, 384 + m * 32:384 + (m + 1) * 32], quarters[:, m * P:(m + 1) * P], sel[:, :],
                                            start=True, stop=True)
                last.then_inc(gates_sum, 1)

            def scores(j):
                slot, kind, h, b = JOBS[j]
                pe.wait_ge(t_out, rounds_by(slot - 1))
                if j:
                    pe.wait_ge(s_read, score_reads(j - 1))
                if kind == "nsa":
                    if j == 0:
                        pe.wait_ge(ck2_out, 2)
                    qt, kt = Q[:, Q_ROT + h, :], Q[:, Q_KS + 2 * b + h // 4, :]
                else:
                    qt, kt = Q[:, Q_MQ[h // 4] + h % 4, :], Q[:, Q_MK[h // 4] + h % 4, :]
                nc.tensor.matmul(b_s[:, 0:P], qt[:, 0:P], kt[:, 0:P], start=True, stop=True)
                last = nc.tensor.matmul(b_s[:, P:3 * P], qt[:, P:S], kt[:, 0:S], start=True, stop=True)
                if kind == "nsa":
                    last = nc.tensor.matmul(b_s[:, 3 * P:3 * P + NCMP], Q[:, Q_RAW + h, b * P:(b + 1) * P],
                                            kcT[:, (h // 4) * CS:(h // 4) * CS + NCMP], start=True, stop=True)
                last.then_inc(scores_done, 1)

            def prob_T(j):
                pe.wait_ge(prob_ready, j + 1)
                if j:
                    pe.wait_ge(pt_out, j)
                for n in range(3):
                    last = nc.tensor.transpose(b_p[:, n * P:(n + 1) * P], prob[:, j % 2, n * P:(n + 1) * P], ident[:, :])
                if JOBS[j][1] == "nsa":
                    last = nc.tensor.transpose(b_p[0:NCMP, 3 * P:4 * P], prob[:, j % 2, 3 * P:3 * P + NCMP], ident[:, :])
                last.then_inc(pt_done, 1)

            def values(j):
                _, kind, h, b = JOBS[j]
                pe.wait_ge(pt_out, j + 1)
                n = heads_done(j) - 1
                if n:
                    pe.wait_ge(o_out, n)
                else:
                    pe.wait_ge(gates_ok, 1)
                if kind == "moba":
                    pe.wait_ge(act_read, act_reads(7 if h < 4 else 10))
                for m in range(MT):
                    prods = []
                    if kind == "moba":
                        for kt in range(m + 1):
                            prods.append((pT[:, j % 2, (m + kt) * P:(m + kt + 1) * P], mv[:, kt, h * HD:(h + 1) * HD]))
                    else:
                        g = h // 4
                        for br in range(2):
                            jb = j - 1 + br
                            for kt in range(m + 1):
                                prods.append((pT[:, jb % 2, (m + kt) * P:(m + kt + 1) * P], nv[:, br, kt, g * HD:(g + 1) * HD]))
                        jb = j - 1 + m
                        prods.append((pT[0:NCMP, jb % 2, 3 * P:4 * P], vc[0:NCMP, g, :]))
                    for n, (a, v) in enumerate(prods):
                        last = nc.tensor.matmul(b_o[:, m * P:(m + 1) * P], a, v, start=n == 0, stop=n == len(prods) - 1)
                last.then_inc(pv_done, 1)

            def y_round_(r):
                half, hg, m = r
                n = Y_NO[r]
                if half == 0:
                    pe.wait_ge(y_scaled, m + 1)
                    if n == 0:
                        pe.wait_ge(t_out, len(ROUNDS))
                    bank_ = b_t
                    if n:
                        pe.wait_ge(yg_done, n)
                else:
                    pe.wait_ge(y_scaled, 2 + m + 1)
                    bank_ = (b_t, b_s, b_p, b_o)[n - 4]
                    if n == 4:
                        pe.wait_ge(yg_done, 4)
                transpose4(bank_, [xo[:, m, half * HW + (hg * HPC + h) * HD:half * HW + (hg * HPC + h + 1) * HD]
                                   for h in range(HPC)], y_round)

            pe.wait_ge(ident_ok, 1)
            x_round_(0)
            x_round_(1)
            pe.wait_ge(grow_in, 16)
            nc.tensor.transpose(b_p[:, 0:KT], grows, ident[0:KT, 0:KT]).then_inc(crows_T, 1)
            x_round_(2)
            x_round_(3)
            for slot in range(NSLOT):
                unit(slot)
                if slot < 2:
                    x_round_(4 + 2 * slot)
                    x_round_(5 + 2 * slot)
                if slot == 1:
                    pe.wait_ge(crow_in, 64)
                    pe.wait_ge(xg_done, 7)
                    nc.tensor.transpose(b_t[:, 0:80], crows, ident[0:80, 0:80]).then_inc(crows_T, 1)
                if slot in ROUNDS:
                    round_(slot)
                if slot in CK_AT:
                    ck_unit(CK_AT[slot])
                if slot in CK_SUM_SLOT:
                    ck_quarters(CK_SUM_SLOT.index(slot))
                if slot in CK2_SLOT:
                    ck_layer2(CK2_SLOT.index(slot))
                if slot == GATE_SLOT:
                    gates()
                if slot == GATE_SLOT + 1:
                    gate_quarters()
                if slot - 3 in JOB_AT and ends_head(JOB_AT[slot - 3]):
                    values(JOB_AT[slot - 3])
                if slot - 2 in JOB_AT:
                    prob_T(JOB_AT[slot - 2])
                if slot in JOB_AT:
                    scores(JOB_AT[slot])
                for r in Y_ROUNDS.get(slot, []):
                    y_round_(r)

        @block.scalar
        def _(act):
            def hi(u):
                act.wait_ge(raw_in[u % RAW], 16 * (u // RAW + (u % RAW > 0)))
                if u >= SPL:
                    act.wait_ge(unit_used, u - SPL + 1)
                nc.scalar.activation(w_hi[:, u % SPL], w_raw[:, u % RAW], ACT.Copy).then_inc(hi_ready, 1)

            def x_hi(r):
                q, m = r // 2, r % 2
                act.wait_ge(xg_done, r + 1)
                nc.scalar.activation(xT_hi[:, q * UK:(q + 1) * UK, m * P:(m + 1) * P],
                                     rope_a[:, r % 2, :].rearrange("p (k t) -> p k t", k=UK), ACT.Copy).then_inc(xhi_done, 1)

            def evac(i):
                kind, _, n = CHUNKS[i]
                act.wait_ge(unit_used, UPC * (i + 1))
                if i == 0:
                    act.wait_ge(rstd_ok, 1)
                if kind == "nq" and n:
                    act.wait_ge(t_round, rounds_by(UPC * i + UPC - 1))
                for m in range(MT):
                    b = proj_b[i % 2][m]
                    if kind in ("kv", "nq"):
                        act.wait_ge(dve_read, dve_reads(i - 1) + 2 * (m + 1))
                    if kind in ("kc", "nq"):
                        nc.scalar.activation(raw_e[:, m, :], b[:, :], ACT.Copy, scale=rstd[:, m:m + 1]).then_inc(act_read, 1)
                    elif kind == "kv":
                        nc.scalar.activation(nv[:, n, m, :], b[:, 2 * HD:4 * HD], ACT.Copy, scale=rstd[:, m:m + 1]).then_inc(act_read, 1)
                    elif kind == "mv":
                        nc.scalar.activation(mv[:, m, n * CW:(n + 1) * CW], b[:, :], ACT.Copy, scale=rstd[:, m:m + 1]).then_inc(act_read, 1)
                    elif kind == "z":
                        z = (rope_a, rope_b)[n % 2]
                        if n >= 2 and m == 0:
                            act.wait_ge(y_done, 2 * (n - 1))
                        if n == 0 and m == 0:
                            act.wait_ge(t_round, len(ROUNDS))
                        nc.scalar.activation(z[:, m, :], b[:, :], ACT.Sigmoid, scale=rstd[:, m:m + 1]).then_inc(act_read, 1)

            def round_out(slot):
                kind, which, _ = ROUNDS[slot]
                if kind == "kc":
                    return
                act.wait_ge(t_round, ROUND_NO[slot] + 1)
                if kind == "kv":
                    dst = Q[:, Q_KS + 2 * which:Q_KS + 2 * which + 2, :]
                    src = b_t[:, :].rearrange("p (g t) -> p g t", g=NG)
                else:
                    n, m = which
                    first = {"rot": Q_ROT + 4 * n, "raw": Q_RAW + 4 * n, "mq": Q_MQ[n], "mk": Q_MK[n]}[kind]
                    dst = Q[:, first:first + HPC, m * P:(m + 1) * P]
                    src = b_t[:, :].rearrange("p (h t) -> p h t", h=HPC)
                nc.scalar.activation(dst, src, ACT.Copy).then_inc(t_out, 1)

            def exps(j):
                act.wait_ge(negmax_ok, j + 1)
                b = j % 2
                for n, (c0, c1) in enumerate(((0, P), (P, 3 * P), (3 * P, 3 * P + NCMP))[:3 if JOBS[j][1] == "nsa" else 2]):
                    last = nc.scalar.activation(prob[:, b, c0:c1], prob[:, b, c0:c1], ACT.Exp, bias=nmx[:, b, n:n + 1],
                                                scale=SCALE, accum_out=sums[:, b, n:n + 1])
                last.then_inc(exp_done, 1)

            def prob_out(j):
                act.wait_ge(pt_done, j + 1)
                last = nc.scalar.activation(pT[:, j % 2, 0:3 * P], b_p[:, 0:3 * P], ACT.Copy)
                if JOBS[j][1] == "nsa":
                    last = nc.scalar.activation(pT[0:NCMP, j % 2, 3 * P:4 * P], b_p[0:NCMP, 3 * P:4 * P], ACT.Copy)
                last.then_inc(pt_out, 1)

            def quarters_out(n):
                act.wait_ge(*((ck_used, 4), (gates_done, 1), (ck_used, 8))[n])
                act.wait_ge(*((cols_ok, 2), (ck_sum, 1), (gates_sum, 1))[n])
                src = (b_s[:, 0:CH], b_o[:, 0:S], b_s[:, CH:2 * CH])[n]
                nc.scalar.activation(quarters, src, ACT.Copy).then_inc(quarters_ok, 1)

            def hidden_exp(kv):
                act.wait_ge(ck_sum, kv + 1)
                nc.scalar.activation(hid_e[:, :, :], b_p[:, 2 * kv * TP:2 * (kv + 1) * TP].rearrange("p (a n) -> p a n", a=2),
                                     ACT.Exp, scale=-1.0).then_inc(ck_exp, 1)

            def ck2_evac(kv):
                act.wait_ge(ck2_done, kv + 1)
                if kv == 0:
                    nc.scalar.activation(kcT[:, :], b_o[:, 0:TP], ACT.Copy).then_inc(ck2_out, 1)
                else:
                    nc.scalar.activation(vc[0:NCMP, :, :], b_o[0:NCMP, HD:3 * HD].rearrange("p (g d) -> p g d", g=NG),
                                         ACT.Copy).then_inc(ck2_out, 1)

            def y_squares(n):
                for m in range(MT):
                    act.wait_ge(y_done, 2 * n + m + 1)
                    if n + m:
                        act.wait_ge(y_sq, 2 * n + m)
                    nc.scalar.activation(junk[:, 0:CW], xo[:, m, n * CW:(n + 1) * CW], ACT.Square,
                                         accum_out=ssy[:, n // 2, m, n % 2:n % 2 + 1]).then_inc(y_sq, 1)

            def y_hi(r):
                half, hg, m = r
                dst = (ymT_hi, xT_hi)[half]
                act.wait_ge(yg_done, Y_NO[r] + 1)
                nc.scalar.activation(dst[:, hg * HPC:(hg + 1) * HPC, m * P:(m + 1) * P],
                                     pT[:, Y_NO[r] % 2, :].rearrange("p (h t) -> p h t", h=HPC), ACT.Copy).then_inc(yhi_done, 1)

            def final_squares(c):
                for m in range(MT):
                    act.wait_ge(dve_read, dve_reads(NC + c - 1) + m + 1)
                    act.wait_ge(*((fin_sq, 2 * c + m) if c + m else (y_sq, 8)))
                    nc.scalar.activation(junk[:, 0:CW], acc[:, m, c * CW:(c + 1) * CW], ACT.Square,
                                         accum_out=ssf[:, m, c:c + 1]).then_inc(fin_sq, 1)

            act.dma_start(grows, g_norm[0].rearrange("(k p) -> k p", p=P)).then_inc(grow_in, 16)

            def w0_part(k):
                act.wait_ge(w0_in[k], 16)
                nc.scalar.activation(w_hi[:, 0, k, :], w_raw[:, 0, k, :], ACT.Copy).then_inc(w0_hi, 1)

            x_hi(0)
            w0_part(0)
            x_hi(1)
            for k in range(1, UK):
                w0_part(k)
            for r0, src in ((0, g_out_moba[0].rearrange("(k p) -> k p", p=P)), (8, g_out_nsa[0].rearrange("(k p) -> k p", p=P)),
                            (16, pe_ck[0]), (48, pe_cv[0])):
                act.dma_start(crows[r0:r0 + src.shape[0], :], src).then_inc(crow_in, 16)
            with nc.allow_non_contiguous_dma(reason="256 positions"):
                act.dma_start(pos_i[:, :], positions[0].rearrange("(m p) -> p m", p=P)).then_inc(trig_in, 16)
            act.dma_start(invf[:, :], inv_freq).then_inc(trig_in, 16)
            with nc.allow_non_contiguous_dma(reason="24 gate columns"):
                act.dma_start(wg[:, :, :], w_in[0, :, COL_G:COL_G + 32].rearrange("(k p) c -> p k c", p=P)).then_inc(wg_in, 16)
            for n, w in enumerate((w_ck2, w_cv2)):
                act.dma_start(w2[:, n, :, :], w[0].rearrange("(t p) d -> p t d", p=P)).then_inc(w2_in, 16)
            x_hi(2)
            x_hi(3)
            hi(1)
            for slot in range(NSLOT):
                if slot + 2 < NSLOT:
                    hi(slot + 2)
                if slot < 2:
                    x_hi(4 + 2 * slot)
                    x_hi(5 + 2 * slot)
                if slot == 1:
                    for q in range(5):
                        act.wait_ge(x_in[q], 16)
                    for m in range(MT):
                        if m:
                            act.wait_ge(sq_done, m)
                        nc.scalar.activation(junk, xo[:, m, :], ACT.Square, accum_out=ssx[:, m:m + 1]).then_inc(sq_done, 1)
                if slot == 3:
                    act.wait_ge(trig_arg, 2)
                    nc.scalar.activation(trig[:, 2, :], trig[:, 2, :], ACT.Sin).then_inc(trig_act, 1)
                    nc.scalar.activation(trig[:, 3, :], trig[:, 3, :], ACT.Sin).then_inc(trig_act, 1)
                if slot in ROUNDS:
                    round_out(slot)
                if slot - 1 in JOB_AT:
                    exps(JOB_AT[slot - 1])
                if slot - 2 in JOB_AT:
                    prob_out(JOB_AT[slot - 2])
                if slot % UPC == UPC - 1 and slot < NPROJ and ACT_READS[KINDS[slot // UPC]]:
                    evac(slot // UPC)
                if slot in (CK_SLOT[3], GATE_SLOT, CK_SLOT[7]):
                    quarters_out((CK_SLOT[3], GATE_SLOT, CK_SLOT[7]).index(slot))
                if slot in CK_SUM_SLOT:
                    hidden_exp(CK_SUM_SLOT.index(slot))
                if slot in CK2_SLOT:
                    ck2_evac(CK2_SLOT.index(slot))
                if slot == GATE_SLOT + 1:
                    act.wait_ge(gates_sum, 1)
                    for m in range(MT):
                        nc.scalar.activation(gate[:, m, :], b_o[:, 384 + m * 32:384 + m * 32 + NGATE], ACT.Exp,
                                             scale=nrstd[:, m:m + 1]).then_inc(gate_exp, 1)
                if slot in (49, 52, 56, 60):
                    y_squares((49, 52, 56, 60).index(slot))
                for r in Y_ROUNDS.get(slot, []):
                    y_hi(r)
                if slot in OUT_DONE:
                    final_squares(OUT_DONE.index(slot))
            act.wait_ge(gmul, 4)
            for m in range(MT):
                act.wait_ge(rstdf_ok, m + 1)
                nc.scalar.activation(acc[:, m, 0:HW], acc[:, m, 0:HW], ACT.Copy, scale=rstdf[:, m:m + 1]).then_inc(fin_act, 1)

        @block.vector
        def _(dve):
            steps = [0]

            def link(ins):
                steps[0] += 1
                ins.then_inc(dve_step, 1)
                dve.wait_ge(dve_step, steps[0])

            def lo(u):
                dve.wait_ge(hi_ready, u)
                nc.vector.tensor_tensor(w_lo[:, u % SPL], w_raw[:, u % RAW], w_hi[:, u % SPL].bitcast(F32),
                                        ALU.subtract).then_inc(lo_ready, 1)

            def x_g(r):
                q, m = r // 2, r % 2
                dve.wait_ge(x_round, r + 1)
                if r >= 2:
                    dve.wait_ge((xlo_even, xlo_odd)[m], q)
                g = ccols[:, q * UK:(q + 1) * UK].unsqueeze(2).to_broadcast([P, UK, P])
                nc.vector.tensor_tensor(rope_a[:, r % 2, :].rearrange("p (k t) -> p k t", k=UK),
                                        xbanks[r % 4][:, :].rearrange("p (k t) -> p k t", k=UK), g, ALU.mult).then_inc(xg_done, 1)

            def x_lo(r):
                q, m = r // 2, r % 2
                dve.wait_ge(xhi_done, r + 1)
                nc.vector.tensor_tensor(xT_lo[:, q * UK:(q + 1) * UK, m * P:(m + 1) * P],
                                        rope_a[:, r % 2, :].rearrange("p (k t) -> p k t", k=UK),
                                        xT_hi[:, q * UK:(q + 1) * UK, m * P:(m + 1) * P].bitcast(F32),
                                        ALU.subtract).then_inc(xlo_odd, 1)

            def angles():
                dve.wait_ge(trig_in, 32)
                link(nc.vector.tensor_copy(pos_f[:, :], pos_i[:, :]))
                ang, n, r, c = (trig[:, i, :] for i in range(4))
                for m in range(MT):
                    link(nc.vector.tensor_scalar(trig[:, 0, m * HALF:(m + 1) * HALF], invf[:, :], pos_f[:, m:m + 1], None, ALU.mult))
                link(nc.vector.tensor_scalar(n, ang, INV_2PI, MAGIC, ALU.mult, ALU.add))
                link(nc.vector.tensor_scalar(n, n, MAGIC, None, ALU.subtract))
                link(nc.vector.scalar_tensor_tensor(r, n, -C1, ang, ALU.mult, ALU.add))
                link(nc.vector.scalar_tensor_tensor(r, n, -C2, r, ALU.mult, ALU.add))
                link(nc.vector.scalar_tensor_tensor(r, n, -C3, r, ALU.mult, ALU.add))
                link(nc.vector.tensor_scalar(r, r, PI, -PI, ALU.min, ALU.max))
                link(nc.vector.scalar_tensor_tensor(c, r, -1.0, r, ALU.mult, ALU.max))
                nc.vector.tensor_scalar(c, c, -1.0, 1.5707963267948966, ALU.mult, ALU.add).then_inc(trig_arg, 2)

            def tables():
                dve.wait_ge(trig_act, 2)
                dve.wait_ge(rstd_ok, 1)
                for m in range(MT):
                    sn, cs = trig[:, 2, m * HALF:(m + 1) * HALF], trig[:, 3, m * HALF:(m + 1) * HALF]
                    nc.vector.tensor_scalar(rope_c[:, m, 0:HALF], cs, rstd[:, m:m + 1], None, ALU.mult).then_inc(tables_ok, 1)
                    nc.vector.tensor_scalar(rope_c[:, m, HALF:HD], cs, rstd[:, m:m + 1], None, ALU.mult).then_inc(tables_ok, 1)
                    nc.vector.tensor_scalar(rope_s[:, m, 0:HALF], sn, rstd[:, m:m + 1], -1.0, ALU.mult, ALU.mult).then_inc(tables_ok, 1)
                    nc.vector.tensor_scalar(rope_s[:, m, HALF:HD], sn, rstd[:, m:m + 1], None, ALU.mult).then_inc(tables_ok, 1)

            def rope(i):
                kind = KINDS[i]
                nh = NG if kind == "kv" else HPC
                dve.wait_ge(unit_used, UPC * (i + 1))
                dve.wait_ge(t_round, rounds_by(UPC * i + UPC - 1))
                dve.wait_ge(rope_sum, rope_sums(i - 1))
                dve.wait_ge(tables_ok, 8)
                for m in range(MT):
                    b = proj_b[i % 2][m][:, 0:nh * HD]
                    heads = b.rearrange("p (h d) -> p h d", h=nh)
                    halves = b.rearrange("p (h a d) -> p h a d", h=nh, a=2)
                    cosb = rope_c[:, m, :].unsqueeze(1).to_broadcast([P, nh, HD])
                    nc.vector.tensor_tensor(rope_a[:, m, 0:nh * HD].rearrange("p (h d) -> p h d", h=nh), heads, cosb,
                                            ALU.mult).then_inc(dve_read, 1)
                    sinb = rope_s[:, m, :].rearrange("p (a d) -> p a d", a=2).unsqueeze(1).to_broadcast([P, nh, 2, HALF])
                    nc.vector.tensor_tensor(rope_b[:, m, 0:nh * HD].rearrange("p (h a d) -> p h a d", h=nh, a=2),
                                            halves[:, :, ::-1, :], sinb, ALU.mult).then_inc(dve_read, 1)

            def kc_out(slot):
                _, m, _ = ROUNDS[slot]
                dve.wait_ge(t_round, ROUND_NO[slot] + 1)
                for kv in range(2):
                    src = b_t[:, kv * 2 * P:(kv + 1) * 2 * P].rearrange("p (a l) -> p a l", l=CS)
                    for half in range(2):
                        pe_ = ccols[:, 32 + kv * CL + half * CS:32 + kv * CL + (half + 1) * CS].unsqueeze(1).unsqueeze(1)
                        dst = kvpe[:, kv, half, :, m * P:(m + 1) * P].rearrange("p g (n l) -> p g n l", l=CS)
                        last = nc.vector.tensor_tensor(dst, src.rearrange("p (g n) l -> p g n l", g=NG),
                                                       pe_.to_broadcast([P, NG, P // CS, CS]), ALU.add)
                last.then_inc(t_out, 1)

            def hidden(kv):
                dve.wait_ge(ck_exp, kv + 1)
                link(nc.vector.tensor_scalar(hid_e[:, :, :], hid_e[:, :, :], 1.0, None, ALU.add))
                link(nc.vector.reciprocal(hid_e[:, :, :], hid_e[:, :, :]))
                nc.vector.tensor_tensor(hidT[:, kv, :, :], b_p[:, 2 * kv * TP:2 * (kv + 1) * TP].rearrange("p (a n) -> p a n", a=2),
                                        hid_e[:, :, :], ALU.mult).then_inc(hid_ready, 1)

            def gates():
                dve.wait_ge(gate_exp, 2)
                link(nc.vector.tensor_scalar(gate[:, :, :], gate[:, :, :], 1.0, None, ALU.add))
                link(nc.vector.reciprocal(gate[:, :, :], gate[:, :, :]))
                v = gate[:, :, :].rearrange("p m (h b) -> p m h b", b=3)
                for b in range(2):
                    for n, (m, br) in enumerate(((0, 1 + b), (1, 1 + b), (b, 0))):
                        last = nc.vector.tensor_copy(gate_j[:, :, b, n], v[:, m, :, br])
                last.then_inc(gates_ok, 1)

            def row_max(j):
                kind, b = JOBS[j][1], JOBS[j][3]
                dve.wait_ge(scores_done, j + 1)
                if j == 0:
                    dve.wait_ge(consts_ok, 4)
                pieces = [(0, P, 0), (P, 3 * P, P)] + ([(3 * P, 3 * P + NCMP, 3 * P + 16 * b)] if kind == "nsa" else [])
                for n, (c0, c1, k0) in enumerate(pieces):
                    nc.vector.tensor_tensor_reduce(out=prob[:, j % 2, c0:c1], in0=b_s[:, c0:c1], in1=mask[:, k0:k0 + c1 - c0],
                                                   scale=1.0, scalar=NEG, op0=ALU.add, op1=ALU.max,
                                                   accum_out=mx[:, j % 2, n:n + 1]).then_inc(s_read, 1)
                dve.wait_ge(s_read, score_reads(j))
                nc.vector.tensor_scalar(nmx[:, j % 2, 0:len(pieces)], mx[:, j % 2, 0:len(pieces)], FLOOR, -SCALE,
                                        ALU.max, ALU.mult).then_inc(negmax_ok, 1)

            def normalise(j):
                _, kind, h, b = JOBS[j]
                n = 3 if kind == "nsa" else 2
                c = coef[:, j % 2, 0:n]
                dve.wait_ge(exp_done, j + 1)
                link(nc.vector.tensor_scalar(c, sums[:, j % 2, 0:n], 1e-30, None, ALU.max))
                link(nc.vector.reciprocal(c, c))
                if kind == "nsa":
                    link(nc.vector.tensor_tensor(c, c, gate_j[:, h, b, 0:3], ALU.mult))
                for i, (c0, c1) in enumerate(((0, P), (P, 3 * P), (3 * P, 3 * P + NCMP))[:n]):
                    last = nc.vector.tensor_scalar(prob[:, j % 2, c0:c1], prob[:, j % 2, c0:c1], coef[:, j % 2, i:i + 1], None, ALU.mult)
                last.then_inc(prob_ready, 1)

            def o_evac(j):
                _, kind, h, _ = JOBS[j]
                col = (0 if kind == "moba" else HW) + h * HD
                dve.wait_ge(pv_done, heads_done(j))
                nc.vector.tensor_copy(xo[:, :, col:col + HD], b_o[:, 0:2 * P].rearrange("p (m d) -> p m d", m=MT)).then_inc(o_out, 1)

            def silu(i):
                n = CHUNKS[i][2]
                z = (rope_a, rope_b)[n % 2]
                for m in range(MT):
                    dve.wait_ge(act_read, act_reads(i - 1) + m + 1)
                    nc.vector.scalar_tensor_tensor(z[:, m, :], proj_b[i % 2][m][:, :], rstd[:, m:m + 1], z[:, m, :],
                                                   ALU.mult, ALU.mult).then_inc(dve_read, 1)

            def y_scale(half):
                dve.wait_ge(rstdy_ok, half + 1)
                for m in range(MT):
                    y = xo[:, m, half * HW:(half + 1) * HW]
                    nc.vector.tensor_scalar(y, y, rstdy[:, half, m:m + 1], None, ALU.mult).then_inc(y_scaled, 1)

            def y_parts(r):
                half, hg, m = r
                n = Y_NO[r]
                bank_ = b_t if half == 0 else (b_t, b_s, b_p, b_o)[n - 4]
                dve.wait_ge(y_round, n + 1)
                dve.wait_ge(pt_out, len(JOBS))
                g0 = 16 + half * NH + hg * HPC
                yg = pT[:, n % 2, :].rearrange("p (h t) -> p h t", h=HPC)
                nc.vector.tensor_tensor(yg, bank_[:, :].rearrange("p (h t) -> p h t", h=HPC),
                                        ccols[:, g0:g0 + HPC].unsqueeze(2).to_broadcast([P, HPC, P]), ALU.mult).then_inc(yg_done, 1)
                dve.wait_ge(yhi_done, n + 1)
                hi_, lo_ = ((ymT_hi, ymT_lo), (xT_hi, xT_lo))[half]
                sl = (slice(None), slice(hg * HPC, (hg + 1) * HPC), slice(m * P, (m + 1) * P))
                nc.vector.tensor_tensor(lo_[sl], yg, hi_[sl].bitcast(F32), ALU.subtract).then_inc(ylo_done, 1)

            def residual(c, m):
                if c == 3 and m == 0:
                    dve.wait_ge(m0_done, 1)
                else:
                    dve.wait_ge(unit_used, OUT_DONE[c] + 1)
                if c == 0:
                    dve.wait_ge(acc_in, 16)
                a = acc[:, m, c * CW:(c + 1) * CW]
                nc.vector.tensor_tensor(a, proj_b[(NC + c) % 2][m][:, :], a, ALU.add).then_inc(dve_read, 1)

            def row_sum(m):
                dve.wait_ge(fin_sq, 7 + m)
                nc.vector.tensor_reduce(ssf1[:, m:m + 1], ssf[:, m, :], mybir.AxisListType.X, ALU.add).then_inc(ssf_ok, 1)

            def final(m):
                dve.wait_ge(rstdf_ok, m + 1)
                r = rstdf[:, m:m + 1]
                nc.vector.tensor_scalar(acc[:, m, 2 * CW:3 * CW], acc[:, m, 2 * CW:3 * CW], r, None, ALU.mult)
                a = acc[:, m, 3 * CW:4 * CW]
                nc.vector.scalar_tensor_tensor(a, a, r, g_fin[:, 3 * CW:4 * CW], ALU.mult, ALU.mult).then_inc(fin_dve, 1)

            dve.wait_ge(crows_T, 1)
            nc.vector.tensor_copy(ccols[:, 0:KT], b_p[:, 0:KT]).then_inc(cols_ok, 1)
            dve.wait_ge(cols_ok, 1)
            x_g(0)
            x_g(1)
            for k in range(UK):
                dve.wait_ge(w0_hi, k + 1)
                nc.vector.tensor_tensor(w_lo[:, 0, k, :], w_raw[:, 0, k, :], w_hi[:, 0, k, :].bitcast(F32),
                                        ALU.subtract).then_inc(w0_lo, 1)
                if k == 0:
                    x_lo(1)
            x_g(2)
            x_g(3)
            lo(1)
            x_lo(3)
            for slot in range(NSLOT):
                if slot + 2 < NSLOT:
                    lo(slot + 2)
                if slot < 2:
                    x_g(4 + 2 * slot)
                    x_g(5 + 2 * slot)
                    x_lo(5 + 2 * slot)
                if slot == 1:
                    dve.wait_ge(crows_T, 2)
                    nc.vector.tensor_copy(ccols[:, KT:], b_t[:, 0:80]).then_inc(cols_ok, 1)
                    dve.wait_ge(cols_ok, 2)
                if slot == 2:
                    angles()
                if slot == 4:
                    tables()
                if slot in ROUNDS and ROUNDS[slot][0] == "kc":
                    kc_out(slot)
                if slot - 1 in JOB_AT:
                    normalise(JOB_AT[slot - 1])
                if slot - 3 in JOB_AT and ends_head(JOB_AT[slot - 3]):
                    o_evac(JOB_AT[slot - 3])
                if slot in JOB_AT:
                    row_max(JOB_AT[slot])
                if slot % UPC == UPC - 1 and slot < NPROJ:
                    if KINDS[slot // UPC] in ROPED:
                        rope(slot // UPC)
                    if KINDS[slot // UPC] == "z":
                        silu(slot // UPC)
                if slot in CK_SUM_SLOT:
                    hidden(CK_SUM_SLOT.index(slot))
                if slot == GATE_SLOT + 1:
                    gates()
                if slot in (53, 61):
                    y_scale((53, 61).index(slot))
                for r in Y_ROUNDS.get(slot, []):
                    y_parts(r)
                if slot in OUT_DONE[:3]:
                    for m in range(MT):
                        residual(OUT_DONE.index(slot), m)
            residual(3, 0)
            dve.wait_ge(gmul, 6)
            row_sum(0)
            residual(3, 1)
            final(0)
            row_sum(1)
            final(1)


_INS = ["x", "positions", "inv_freq", "w_in", "g_norm", "pe_ck", "pe_cv", "w_ck1", "w_ck2", "w_cv1", "w_cv2",
        "g_out_moba", "g_out_nsa", "w_out", "g_final"]


def kernel(**inputs):
    import numpy as _np
    import concourse.bacc as _bacc
    from concourse import mybir as _mybir
    from concourse.bass_utils import run_bass_kernel_spmd as _run

    freq = 1.0 / (_np.float32(10000.0) ** (_np.arange(0, HD, 2, dtype=_np.float32) / _np.float32(HD)))
    inv_freq = _np.ascontiguousarray(_np.broadcast_to(freq.astype(_np.float32), (P, HALF)))
    nc = _bacc.Bacc("TRN2", target_bir_lowering=False, num_devices=1)
    arrays, args = {}, []
    for name in _INS:
        a = inv_freq if name == "inv_freq" else _np.ascontiguousarray(inputs[name])
        arrays[f"in_{name}_dram"] = a
        args.append(nc.dram_tensor(f"in_{name}_dram", a.shape, _mybir.dt.from_np(a.dtype), kind="ExternalInput").ap())
    args.append(nc.dram_tensor("out_dram", (1, S, D), _mybir.dt.float32, kind="ExternalOutput").ap())
    build_layer(nc, *args)
    r = _run(nc, [arrays], core_ids=[0])
    return r.results[0]["out_dram"]
```

```python
import concourse.bass as bass
from concourse import mybir
from contextlib import ExitStack


S, D, P, HD = 256, 2048, 128, 128
MT = S // P
KT = D // P
NH = 8
HW = NH * HD
CW = 512
UK = 4
UPC = KT // UK
HPC = CW // HD
NG, NGATE = 2, 24
NCMP, CL, CS, CH = 15, 32, 16, 256
SCALE = HD ** -0.5
EPS = 1e-6
NEG = -3.0e38
FLOOR = -1.0e38
HALF = HD // 2

COL_MQ, COL_MK, COL_MV, COL_MZ = 0, HW, 2 * HW, 3 * HW
COL_NQ = 4 * HW
COL_KC = 5 * HW
COL_KS, COL_KW, COL_G = COL_KC + 512, COL_KC + 1024, COL_KC + 1536
COL_NZ = COL_G + NGATE
CHUNKS = [("kc", COL_KC, 0), ("kv", COL_KS, 0), ("kv", COL_KW, 1), ("nq", COL_NQ, 0), ("nq", COL_NQ + CW, 1),
          ("mq", COL_MQ, 0), ("mk", COL_MK, 0), ("mv", COL_MV, 0), ("mq", COL_MQ + CW, 1),
          ("mk", COL_MK + CW, 1), ("mv", COL_MV + CW, 1),
          ("z", COL_MZ, 0), ("z", COL_MZ + CW, 1), ("z", COL_NZ, 2), ("z", COL_NZ + CW, 3)]
NC = len(CHUNKS)
NPROJ = NC * UPC
OUT_UNITS = [(0, 0), (0, 1), (1, 0), (1, 1), (0, 2), (1, 2), (0, 3), (1, 3)] + [(c, g) for c in (2, 3) for g in range(4)]
NSLOT = NPROJ + len(OUT_UNITS)
OUT_DONE = [NPROJ + max(i for i, u in enumerate(OUT_UNITS) if u[0] == c) for c in range(3)]
OUT_SLOT = OUT_DONE[:2] + [OUT_DONE[2] + 2]
RAW, SPL = 3, 3
NBUSY = 15
X_ROUNDS_AT = {(0, 2): 2, (1, 2): 4, (1, 5): 6}
FIRST = 3
LAST = NSLOT - UPC

ACT_READS = {"kc": 2, "kv": 2, "nq": 2, "mq": 0, "mk": 0, "mv": 2, "z": 2, "out": 0}
DVE_READS = {"kc": 0, "kv": 4, "nq": 4, "mq": 4, "mk": 4, "mv": 0, "z": 2, "out": 2}
KINDS = [c[0] for c in CHUNKS] + ["out"] * 4
ROPED = ("kv", "nq", "mq", "mk")


def act_reads(i):
    return sum(ACT_READS[k] for k in KINDS[:i + 1])


def dve_reads(i):
    return sum(DVE_READS[k] for k in KINDS[:i + 1])


def rope_sums(i):
    return 2 * sum(k in ROPED for k in KINDS[:i + 1])


Q_ROT, Q_RAW, Q_KS, Q_MQ, Q_MK = 0, 8, 16, [20, 0], [24, 8]


def transpose_rounds():
    out = {}
    for i, (kind, _, n) in enumerate(CHUNKS):
        s = UPC * i + UPC
        if kind == "kc":
            out[s], out[s + 1] = ("kc", 0, i), ("kc", 1, i)
        elif kind == "kv":
            out[s] = ("kv", n, i)
        elif kind == "nq":
            for k, m in ((0, 0), (0, 1), (1, 0), (1, 1)):
                out[s + 2 * k + m] = (("rot", "raw")[k], (n, m), i)
        elif kind in ("mq", "mk"):
            out[s], out[s + 1] = (kind, (n, 0), i), (kind, (n, 1), i)
    return out


ROUNDS = transpose_rounds()
ROUND_NO = {s: n for n, s in enumerate(sorted(ROUNDS))}


def rounds_by(slot):
    return sum(s <= slot for s in ROUNDS)


JOBS = [(20 + 2 * h + b, "nsa", h, b) for h in range(8) for b in range(2)] + \
       [(36 + h, "moba", h, 0) for h in range(4)] + [(42 + h, "moba", 4 + h, 0) for h in range(4)]
JOB_AT = {j[0]: n for n, j in enumerate(JOBS)}
LAST_JOB_SLOT = JOBS[-1][0]


def score_reads(j):
    return sum(3 if JOBS[i][1] == "nsa" else 2 for i in range(j + 1))


def ends_head(j):
    return JOBS[j][1] == "moba" or JOBS[j][3] == 1


def heads_done(j):
    return sum(ends_head(i) for i in range(j + 1))


CK_SLOT = [6, 7, 9, 10, 12, 13, 15, 16]
CK_AT = {s: c for c, s in enumerate(CK_SLOT)}
CK_SUM_SLOT = [11, 17]
CK2_SLOT = [12, 18]
GATE_SLOT = 13
TP = 2 * CS
Y_ROUNDS = {54: [(0, 0, 0)], 55: [(0, 0, 1)], 56: [(0, 1, 0)], 57: [(0, 1, 1)],
            62: [(1, 0, 0), (1, 0, 1)], 63: [(1, 1, 0), (1, 1, 1)]}
Y_NO = {r: n for n, r in enumerate(r for s in sorted(Y_ROUNDS) for r in Y_ROUNDS[s])}

INV_2PI = 0.15915494309189535
MAGIC = 12582912.0
C1 = 6.28125
C2 = 0.0019350051879882812
C3 = 6.283185307179586 - C1 - C2
PI = 3.1415925


def build_layer(nc, x, positions, inv_freq, w_in, g_norm, pe_ck, pe_cv, w_ck1, w_ck2, w_cv1, w_cv2,
                g_out_moba, g_out_nsa, w_out, g_final, out):
    F32, F32R, BF16, I32 = mybir.dt.float32, mybir.dt.float32r, mybir.dt.bfloat16, mybir.dt.int32
    ALU, ACT = mybir.AluOpType, mybir.ActivationFunctionType

    with ExitStack() as ctx:
        def sb(name, shape, dt=F32):
            return ctx.enter_context(nc.sbuf_tensor(name, shape, dt))

        def sem(name):
            return ctx.enter_context(nc.semaphore(name))

        xo = sb("xo", [P, MT, D])
        xT_hi, xT_lo = sb("xT_hi", [P, KT, S], F32R), sb("xT_lo", [P, KT, S], F32R)
        ymT_hi, ymT_lo = sb("ymT_hi", [P, NH, S], F32R), sb("ymT_lo", [P, NH, S], F32R)
        w_raw = sb("w_raw", [P, RAW, UK, CW])
        w_hi, w_lo = sb("w_hi", [P, SPL, UK, CW], F32R), sb("w_lo", [P, SPL, UK, CW], F32R)
        Q = sb("Q", [P, 28, S])
        acc = Q[:, 0:16, :].rearrange("p a b -> p (a b)").rearrange("p (m d) -> p m d", m=MT)
        g_fin = Q[:, 16:24, :].rearrange("p a b -> p (a b)")
        KV8 = sb("KV8", [P, D + CS])
        kvpe = KV8[:, 0:D].rearrange("p (v h g t) -> p v h g t", v=2, h=2, g=NG)
        mv = KV8[:, 0:D].rearrange("p (m c) -> p m c", m=MT)
        nv = sb("nv", [P, 2, MT, 2 * HD])
        rope_a, rope_b = sb("rope_a", [P, MT, CW]), sb("rope_b", [P, MT, CW])
        raw_e = sb("raw_e", [P, MT, CW])
        junk = raw_e[:, :, :].rearrange("p m c -> p (m c)").bitcast(BF16)
        prob = sb("prob", [P, 2, 400])
        w2 = prob[:, :, :].rearrange("p a b -> p (a b)")[:, 0:4 * HD].rearrange("p (v t d) -> p v t d", v=2, t=2)
        pT = sb("pT", [P, 2, 512])
        trig = pT[:, 0, :].rearrange("p (a c) -> p a c", a=4)
        crows, grows = pT[0:80, 1, 0:P], pT[0:16, 1, P:2 * P]
        quarters = pT[:, 1, 0:CH]
        ident = sb("ident", [P, P])
        mask = sb("mask", [P, 3 * P + 2 * NCMP + 2])
        ccols = sb("ccols", [P, 96])
        invf, pos_i, pos_f = sb("invf", [P, HALF]), sb("pos_i", [P, MT], I32), sb("pos_f", [P, MT])
        rope_c, rope_s = sb("rope_c", [P, MT, HD]), sb("rope_s", [P, MT, HD])
        ssx, rstd, nrstd = sb("ssx", [P, MT]), sb("rstd", [P, MT]), sb("nrstd", [P, MT])
        half_c = sb("half_c", [P, MT])
        mx, sums, coef = sb("mx", [P, 2, 4]), sb("sums", [P, 2, 4]), sb("coef", [P, 2, 4])
        nmx = sb("nmx", [P, 2, 4])
        wg = sb("wg", [P, KT, 32])
        sel = sb("sel", [P, 32])
        gate, gate_j = sb("gate", [P, MT, NGATE]), sb("gate_j", [P, NH, 2, 4])
        hid_e, hidT = sb("hid_e", [P, 2, TP]), sb("hidT", [P, 2, 2, TP])
        kcT, vc = sb("kcT", [P, CS + P]), sb("vc", [16, NG, HD])
        ssy, rstdy = sb("ssy", [P, 2, MT, 2]), sb("rstdy", [P, 2, MT])
        ssf, ssf1, rstdf = sb("ssf", [P, MT, 4]), sb("ssf1", [P, MT]), sb("rstdf", [P, MT])

        def bank(name):
            return ctx.enter_context(nc.psum_tensor(name, [P, 512], F32))

        proj_b = [[bank(f"proj{i}{m}") for m in range(MT)] for i in range(2)]
        b_s, b_o, b_t, b_p = bank("b_s"), bank("b_o"), bank("b_t"), bank("b_p")
        xbanks = [b_s, b_o, b_t, b_p]

        x_in = [sem(f"x_in{q}") for q in range(5)]
        first_in = [sem(f"first_in{n}") for n in range(FIRST * UK)]
        raw_in = [sem(f"raw_in{i}") for i in range(RAW)]
        ck_in = [sem(f"ck_in{i}") for i in range(2)]
        grow_in, crow_in, trig_in, wg_in, w2_in = sem("grow_in"), sem("crow_in"), sem("trig_in"), sem("wg_in"), sem("w2_in")
        acc_in, gfin_in, out_in = sem("acc_in"), sem("gfin_in"), sem("out_in")
        ident_ok, consts_ok, pool_step = sem("ident_ok"), sem("consts_ok"), sem("pool_step")
        sel_ok, xlo_even, rstd_ok, rope_sum, y_done = sem("sel_ok"), sem("xlo_even"), sem("rstd_ok"), sem("rope_sum"), sem("y_done")
        rstdy_ok, rstdf_ok = sem("rstdy_ok"), sem("rstdf_ok")
        gmul = sem("gmul")
        crows_T, x_round, unit_used, t_round = sem("crows_T"), sem("x_round"), sem("unit_used"), sem("t_round")
        ck_used, ck_sum, ck2_done = sem("ck_used"), sem("ck_sum"), sem("ck2_done")
        gates_done, gates_sum, last_done = sem("gates_done"), sem("gates_sum"), sem("last_done")
        scores_done, pt_done, pv_done, y_round = sem("scores_done"), sem("pt_done"), sem("pv_done"), sem("y_round")
        hi_ready, xhi_done, sq_done, trig_act = sem("hi_ready"), sem("xhi_done"), sem("sq_done"), sem("trig_act")
        act_read, ck_exp, ck2_out, gate_exp = sem("act_read"), sem("ck_exp"), sem("ck2_out"), sem("gate_exp")
        first_hi, quarters_ok, exp_done, pt_out, y_sq = sem("first_hi"), sem("quarters_ok"), sem("exp_done"), sem("pt_out"), sem("y_sq")
        yhi_done, fin_sq, fin_act = sem("yhi_done"), sem("fin_sq"), sem("fin_act")
        cols_ok, xg_done, lo_ready, dve_read = sem("cols_ok"), sem("xg_done"), sem("lo_ready"), sem("dve_read")
        dve_step, trig_arg, tables_ok = sem("dve_step"), sem("trig_arg"), sem("tables_ok")
        hid_ready, first_lo, gates_ok, xlo_odd = sem("hid_ready"), sem("first_lo"), sem("gates_ok"), sem("xlo_odd")
        s_read, negmax_ok, prob_ready, o_out = sem("s_read"), sem("negmax_ok"), sem("prob_ready"), sem("o_out")
        y_scaled, yg_done, ylo_done, ssf_ok, fin_dve = sem("y_scaled"), sem("yg_done"), sem("ylo_done"), sem("ssf_ok"), sem("fin_dve")
        t_out = sem("t_out")

        block = ctx.enter_context(nc.Block())

        def x_buf(r):
            return (rope_a, rope_b)[r // 2 % 2][:, r % 2, :].rearrange("p (k t) -> p k t", k=UK)

        def unit_src(u):
            if u < NPROJ:
                col, g = CHUNKS[u // UPC][1], u % UPC
                src = w_in[0, g * UK * P:(g + 1) * UK * P, col:col + CW]
            else:
                c, g = OUT_UNITS[u - NPROJ]
                src = w_out[0, g * UK * P:(g + 1) * UK * P, c * CW:(c + 1) * CW]
            return src.rearrange("(k p) c -> p k c", p=P)

        def split_of(u):
            if u == NSLOT - 1:
                return [t[:, NH:KT, :].rearrange("p a t -> p (a t)").rearrange("p (k c) -> p k c", k=UK) for t in (xT_hi, xT_lo)]
            return w_hi[:, u % SPL], w_lo[:, u % SPL]

        @block.sync
        def _(sp):
            def x_quarter(q):
                if q == 0:
                    for m in range(MT):
                        sp.dma_start(xo[:, m, 0:CW], x[0, m * P:(m + 1) * P, 0:CW]).then_inc(x_in[4 * m], 16)
                else:
                    sp.dma_start(xo[:, :, q * CW:(q + 1) * CW],
                                 x[0, :, q * CW:(q + 1) * CW].rearrange("(m p) c -> p m c", p=P)).then_inc(x_in[q], 16)

            def unit(u):
                if u < 2 * FIRST:
                    sp.wait_ge(first_lo, UK * (u - RAW + 1))
                else:
                    sp.wait_ge(lo_ready, u - RAW - FIRST + 1)
                sp.dma_start(w_raw[:, u % RAW], unit_src(u)).then_inc(raw_in[u % RAW], 16)

            def first_unit(u):
                for k in range(UK):
                    sp.dma_start(w_raw[:, u, k, :], unit_src(u)[:, k, :]).then_inc(first_in[u * UK + k], 16)

            def ck_unit(c):
                if c == 0:
                    sp.wait_ge(sq_done, 2)
                    sp.wait_ge(x_round, 8)
                if c >= 2:
                    sp.wait_ge(ck_used, c - 1)
                w = (w_ck1, w_cv1)[c // 4]
                l0 = (c % 4) * 8
                sp.dma_start(xo[:, c % 2, :].rearrange("p (l h) -> p l h", l=8),
                             w[0, l0 * HD:(l0 + 8) * HD, :].rearrange("(l d) h -> d l h", d=HD)).then_inc(ck_in[c % 2], 16)

            x_quarter(0)
            for u in range(FIRST):
                first_unit(u)
                x_quarter(u + 1)
            ck_next = 0
            for u in range(RAW, NSLOT):
                unit(u)
                while ck_next < 8 and u >= CK_SLOT[ck_next] and u >= 6:
                    ck_unit(ck_next)
                    ck_next += 1
                if u == 54:
                    sp.wait_ge(scores_done, len(JOBS))
                    sp.dma_start(acc, x[0].rearrange("(m p) c -> p m c", p=P)).then_inc(acc_in, 16)
                if u == 56:
                    sp.dma_start(g_fin, g_final.rearrange("(a d) -> a d", a=1).to_broadcast([P, D])).then_inc(gfin_in, 16)
            for m in range(MT):
                for h, done in enumerate((fin_act, fin_dve)):
                    sp.wait_ge(done, m + 1)
                    sp.dma_start(out[0, m * P:(m + 1) * P, h * HW:(h + 1) * HW], acc[:, m, h * HW:(h + 1) * HW]).then_inc(out_in, 16)
            sp.wait_ge(out_in, 32 * MT)

        @block.gpsimd
        def _(pool):
            steps = [0]

            def link(ins):
                steps[0] += 1
                ins.then_inc(pool_step, 1)
                pool.wait_ge(pool_step, steps[0])

            link(nc.gpsimd.memset(ident[:, :], 0.0))
            nc.gpsimd.affine_select(out=ident[:, :], in_=ident[:, :], compare_op=ALU.not_equal, fill=1.0, base=0,
                                    pattern=[[-1, P]], channel_multiplier=1).then_inc(ident_ok, 1)
            nc.gpsimd.memset(half_c[:, :], -0.5)
            link(nc.gpsimd.memset(mask[:, :], 0.0))
            for c0, n, step, base in ((0, P, -1, 0), (2 * P, P, -1, 0), (3 * P, NCMP, -CS, 1 - CL), (3 * P + 16, NCMP, -CS, P + 1 - CL)):
                nc.gpsimd.affine_select(out=mask[:, c0:c0 + n], in_=mask[:, c0:c0 + n], compare_op=ALU.is_ge, fill=NEG,
                                        base=base, pattern=[[step, n]], channel_multiplier=1).then_inc(consts_ok, 1)
            link(nc.gpsimd.memset(sel[:, :], 0.0))
            for n in range(4):
                link(nc.gpsimd.affine_select(out=sel[:, :], in_=sel[:, :], compare_op=ALU.not_equal, fill=1.0, base=-32 * n,
                                             pattern=[[-1, 32]], channel_multiplier=1))
            nc.gpsimd.memset(kcT[:, TP:], 0.0).then_inc(sel_ok, 1)
            nc.gpsimd.memset(KV8[:, D:], 0.0).then_inc(sel_ok, 1)
            for r in range(0, 8, 2):
                q, m = r // 2, r % 2
                pool.wait_ge(xhi_done, r + 1)
                nc.gpsimd.tensor_tensor(xT_lo[:, q * UK:(q + 1) * UK, m * P:(m + 1) * P],
                                        x_buf(r),
                                        xT_hi[:, q * UK:(q + 1) * UK, m * P:(m + 1) * P].bitcast(F32),
                                        ALU.subtract).then_inc(xlo_even, 1)
            pool.wait_ge(sq_done, 2)
            link(nc.gpsimd.tensor_scalar(ssx[:, :], ssx[:, :], 1.0 / D, EPS, ALU.mult, ALU.add))
            nc.gpsimd.tensor_tensor(rstd[:, :], ssx[:, :], half_c[:, :], ALU.pow).then_inc(rstd_ok, 1)
            pool.wait_ge(rstd_ok, 1)
            nc.gpsimd.tensor_scalar(nrstd[:, :], rstd[:, :], -1.0, None, ALU.mult).then_inc(rstd_ok, 1)
            for i, kind in enumerate(KINDS[:NC]):
                if kind in ROPED:
                    w = 2 * HD if kind == "kv" else CW
                    for m in range(MT):
                        pool.wait_ge(dve_read, dve_reads(i - 1) + 2 * (m + 1))
                        nc.gpsimd.tensor_tensor(rope_a[:, m, 0:w], rope_a[:, m, 0:w], rope_b[:, m, 0:w],
                                                ALU.add).then_inc(rope_sum, 1)
                elif kind == "z":
                    n = CHUNKS[i][2]
                    z = (rope_a, rope_b)[n % 2]
                    if n == 0:
                        pool.wait_ge(o_out, 2 * NH)
                    for m in range(MT):
                        pool.wait_ge(dve_read, dve_reads(i - 1) + m + 1)
                        nc.gpsimd.tensor_tensor(xo[:, m, n * CW:(n + 1) * CW], xo[:, m, n * CW:(n + 1) * CW],
                                                z[:, m, :], ALU.mult).then_inc(y_done, 1)
                    if n % 2:
                        h = n // 2
                        pool.wait_ge(y_sq, 4 * (h + 1))
                        link(nc.gpsimd.tensor_tensor(rstdy[:, h, :], ssy[:, h, :, 0], ssy[:, h, :, 1], ALU.add))
                        link(nc.gpsimd.tensor_scalar(rstdy[:, h, :], rstdy[:, h, :], 1.0 / HW, EPS, ALU.mult, ALU.add))
                        nc.gpsimd.tensor_tensor(rstdy[:, h, :], rstdy[:, h, :], half_c[:, :], ALU.pow).then_inc(rstdy_ok, 1)
            pool.wait_ge(gfin_in, 16)
            for c in range(3):
                for m in range(MT):
                    pool.wait_ge(fin_sq, 2 * c + m + 1)
                    nc.gpsimd.tensor_tensor(acc[:, m, c * CW:(c + 1) * CW], acc[:, m, c * CW:(c + 1) * CW],
                                            g_fin[:, c * CW:(c + 1) * CW], ALU.mult).then_inc(gmul, 1)
            pool.wait_ge(ssf_ok, 2)
            for m in range(MT):
                pool.wait_ge(fin_sq, 7 + m)
                one = slice(m, m + 1)
                link(nc.gpsimd.tensor_scalar(ssf1[:, one], ssf[:, m, 3:4], 1.0 / D, ssf1[:, one], ALU.mult, ALU.add))
                nc.gpsimd.tensor_tensor(rstdf[:, one], ssf1[:, one], half_c[:, one], ALU.pow).then_inc(rstdf_ok, 1)

        @block.tensor
        def _(pe):
            def transpose4(bank_, srcs, done):
                for n, src in enumerate(srcs):
                    last = nc.tensor.transpose(bank_[:, n * P:(n + 1) * P], src, ident[:, :])
                last.then_inc(done, 1)

            def x_round_(r):
                q, m = r // 2, r % 2
                pe.wait_ge(x_in[4 * m if q == 0 else q], 16)
                if r == 3:
                    pe.wait_ge(cols_ok, 1)
                if r >= 4:
                    pe.wait_ge(xg_done, r - 3)
                transpose4(xbanks[r % 4], [xo[:, m, (q * UK + k) * P:(q * UK + k + 1) * P] for k in range(UK)], x_round)

            def three_products(dst, a_hi, a_lo, b_hi, b_lo, first, last):
                nc.tensor.matmul(dst, a_hi, b_hi, start=first, stop=False)
                nc.tensor.matmul(dst, a_hi, b_lo, start=False, stop=False)
                return nc.tensor.matmul(dst, a_lo, b_hi, start=False, stop=last)

            def operands(u, m, k):
                if u < NPROJ:
                    c, row, sh, sl = u // UPC, (u % UPC) * UK + k, xT_hi, xT_lo
                else:
                    c, g = OUT_UNITS[u - NPROJ]
                    row, sh, sl = (g * UK + k, ymT_hi, ymT_lo) if g < 2 else ((g - 2) * UK + k, xT_hi, xT_lo)
                    c += NC
                tok = slice(m * P, (m + 1) * P)
                wh, wl = split_of(u)
                return proj_b[c % 2][m][:, :], sh[:, row, tok], sl[:, row, tok], wh[:, k, :], wl[:, k, :]

            def bank_free(c):
                if c >= 2:
                    pe.wait_ge(act_read, act_reads(c - 2))
                    pe.wait_ge(dve_read, dve_reads(c - 2))

            def unit(u):
                if u < NPROJ:
                    c, g = u // UPC, u % UPC
                    if u < UPC:
                        pe.wait_ge(xlo_even, u + 1)
                        pe.wait_ge(xlo_odd, u + 1)
                else:
                    c, g = OUT_UNITS[u - NPROJ]
                    c += NC
                    pe.wait_ge(ylo_done, 4 if g < 2 else 2 * g + 2)
                if g == 0:
                    bank_free(c)
                if u >= FIRST:
                    pe.wait_ge(lo_ready, u - FIRST + 1)
                order = [(m, k) for m in range(MT) for k in range(UK)]
                if u < FIRST:
                    order = [(m, k) for k in range(UK) for m in range(MT)]
                for n, (m, k) in enumerate(order):
                    if u < FIRST and m == 0:
                        pe.wait_ge(first_lo, u * UK + k + 1)
                    if (u, n) in X_ROUNDS_AT:
                        x_round_(X_ROUNDS_AT[u, n])
                        x_round_(X_ROUNDS_AT[u, n] + 1)
                    last = three_products(*operands(u, m, k), g == 0 and k == 0, g == UPC - 1 and k == UK - 1)
                last.then_inc(unit_used, 1)

            def last_chunk():
                bank_free(NC + 3)
                for m in range(MT):
                    for g in range(UPC):
                        if m == 0:
                            pe.wait_ge(lo_ready, LAST + g - FIRST + 1)
                        for k in range(UK):
                            last = three_products(*operands(LAST + g, m, k), g == 0 and k == 0, g == UPC - 1 and k == UK - 1)
                    last.then_inc(last_done, 1)

            def round_(slot):
                kind, which, i = ROUNDS[slot]
                no = ROUND_NO[slot]
                if no:
                    pe.wait_ge(t_out, no)
                else:
                    pe.wait_ge(cols_ok, 2)
                if kind == "kc":
                    pe.wait_ge(act_read, act_reads(i - 1) + which + 1)
                    srcs = [raw_e[:, which, h * HD:(h + 1) * HD] for h in range(HPC)]
                elif kind == "kv":
                    pe.wait_ge(rope_sum, rope_sums(i))
                    srcs = [rope_a[:, m, g * HD:(g + 1) * HD] for g in range(NG) for m in range(MT)]
                elif kind == "raw":
                    pe.wait_ge(act_read, act_reads(i))
                    srcs = [raw_e[:, which[1], h * HD:(h + 1) * HD] for h in range(HPC)]
                else:
                    pe.wait_ge(rope_sum, rope_sums(i - 1) + which[1] + 1)
                    srcs = [rope_a[:, which[1], h * HD:(h + 1) * HD] for h in range(HPC)]
                transpose4(b_t, srcs, t_round)

            def ck_unit(c):
                kv = c // 4
                if c == 0:
                    pe.wait_ge(t_out, 2)
                    pe.wait_ge(sel_ok, 2)
                pe.wait_ge(ck_in[c % 2], 16 * (c // 2 + 1))
                if c == 4:
                    pe.wait_ge(quarters_ok, 1)
                w = xo[:, c % 2, :].rearrange("p (l h) -> p l h", l=8)
                for l8 in range(8):
                    l, j = (c % 4) * 8 + l8, l8 % 4
                    t0 = (2 * kv + l // CS) * NG * S + l
                    last = nc.tensor.matmul(b_s[32 * j:32 * j + 32, kv * CH:(kv + 1) * CH],
                                            KV8[:, t0:t0 + CS * (TP - 1) + 1:CS], w[:, l8, :], start=l < 4, stop=l >= CL - 4)
                last.then_inc(ck_used, 1)

            def ck_quarters(kv):
                pe.wait_ge(quarters_ok, (1, 3)[kv])
                for ht in range(2):
                    last = nc.tensor.matmul(b_p[:, (2 * kv + ht) * TP:(2 * kv + ht + 1) * TP], quarters[:, ht * P:(ht + 1) * P],
                                            sel[:, :], start=True, stop=True)
                last.then_inc(ck_sum, 1)

            def ck_layer2(kv):
                if kv == 0:
                    pe.wait_ge(w2_in, 32)
                pe.wait_ge(hid_ready, kv + 1)
                if kv:
                    pe.wait_ge(gate_exp, 2)
                if kv == 0:
                    for ht in range(2):
                        last = nc.tensor.matmul(b_o[:, 0:TP], w2[:, 0, ht, :], hidT[:, 0, ht, :],
                                                start=ht == 0, stop=ht == 1)
                else:
                    for g in range(NG):
                        for ht in range(2):
                            last = nc.tensor.matmul(b_o[0:NCMP, (g + 1) * HD:(g + 2) * HD],
                                                    hidT[:, 1, ht, g * CS:g * CS + NCMP], w2[:, 1, ht, :],
                                                    start=ht == 0, stop=ht == 1)
                last.then_inc(ck2_done, 1)

            def gates():
                pe.wait_ge(wg_in, 16)
                pe.wait_ge(ck2_out, 1)
                for n, part in enumerate((xT_hi, xT_lo)):
                    for k in range(KT):
                        j = k % 4
                        last = nc.tensor.matmul(b_o[32 * j:32 * j + 32, 0:S], wg[:, k, :], part[:, k, :].bitcast(F32),
                                                start=n == 0 and k < 4, stop=n == 1 and k >= KT - 4)
                last.then_inc(gates_done, 1)

            def gate_quarters():
                pe.wait_ge(quarters_ok, 2)
                for m in range(MT):
                    last = nc.tensor.matmul(b_o[:, 384 + m * 32:384 + (m + 1) * 32], quarters[:, m * P:(m + 1) * P], sel[:, :],
                                            start=True, stop=True)
                last.then_inc(gates_sum, 1)

            def scores(j):
                slot, kind, h, b = JOBS[j]
                pe.wait_ge(t_out, rounds_by(slot - 1))
                if j:
                    pe.wait_ge(s_read, score_reads(j - 1))
                if kind == "nsa":
                    if j == 0:
                        pe.wait_ge(ck2_out, 2)
                    qt, kt = Q[:, Q_ROT + h, :], Q[:, Q_KS + 2 * b + h // 4, :]
                else:
                    qt, kt = Q[:, Q_MQ[h // 4] + h % 4, :], Q[:, Q_MK[h // 4] + h % 4, :]
                nc.tensor.matmul(b_s[:, 0:P], qt[:, 0:P], kt[:, 0:P], start=True, stop=True)
                last = nc.tensor.matmul(b_s[:, P:3 * P], qt[:, P:S], kt[:, 0:S], start=True, stop=True)
                if kind == "nsa":
                    last = nc.tensor.matmul(b_s[:, 3 * P:4 * P], Q[:, Q_RAW + h, b * P:(b + 1) * P],
                                            kcT[:, (h // 4) * CS:(h // 4) * CS + P], start=True, stop=True)
                last.then_inc(scores_done, 1)

            def prob_T(j):
                pe.wait_ge(prob_ready, j + 1)
                if j:
                    pe.wait_ge(pt_out, j)
                for n in range(3):
                    last = nc.tensor.transpose(b_p[:, n * P:(n + 1) * P], prob[:, j % 2, n * P:(n + 1) * P], ident[:, :])
                if JOBS[j][1] == "nsa":
                    last = nc.tensor.transpose(b_p[0:NCMP, 3 * P:4 * P], prob[:, j % 2, 3 * P:3 * P + NCMP], ident[:, :])
                last.then_inc(pt_done, 1)

            def values(j):
                _, kind, h, b = JOBS[j]
                pe.wait_ge(pt_out, j + 1)
                n = heads_done(j) - 1
                if n:
                    pe.wait_ge(o_out, n)
                else:
                    pe.wait_ge(gates_ok, 1)
                if kind == "moba":
                    pe.wait_ge(act_read, act_reads(7 if h < 4 else 10))
                for m in range(MT):
                    prods = []
                    if kind == "moba":
                        for kt in range(m + 1):
                            prods.append((pT[:, j % 2, (m + kt) * P:(m + kt + 1) * P], mv[:, kt, h * HD:(h + 1) * HD]))
                    else:
                        g = h // 4
                        for br in range(2):
                            jb = j - 1 + br
                            for kt in range(m + 1):
                                prods.append((pT[:, jb % 2, (m + kt) * P:(m + kt + 1) * P], nv[:, br, kt, g * HD:(g + 1) * HD]))
                        jb = j - 1 + m
                        prods.append((pT[0:NCMP, jb % 2, 3 * P:4 * P], vc[0:NCMP, g, :]))
                    for n, (a, v) in enumerate(prods):
                        last = nc.tensor.matmul(b_o[:, m * P:(m + 1) * P], a, v, start=n == 0, stop=n == len(prods) - 1)
                last.then_inc(pv_done, 1)

            def y_round_(r):
                half, hg, m = r
                n = Y_NO[r]
                if half == 0:
                    pe.wait_ge(y_scaled, m + 1)
                    if n == 0:
                        pe.wait_ge(t_out, len(ROUNDS))
                    bank_ = b_t
                    if n:
                        pe.wait_ge(yg_done, n)
                else:
                    pe.wait_ge(y_scaled, 2 + m + 1)
                    bank_ = (b_t, b_s, b_p, b_o)[n - 4]
                    if n == 4:
                        pe.wait_ge(yg_done, 4)
                transpose4(bank_, [xo[:, m, half * HW + (hg * HPC + h) * HD:half * HW + (hg * HPC + h + 1) * HD]
                                   for h in range(HPC)], y_round)

            def keep_busy(n):
                for _ in range(n):
                    nc.tensor.matmul(b_t[:, 0:P], ident[:, :], ident[:, :], start=True, stop=True)

            pe.wait_ge(ident_ok, 1)
            keep_busy(4)
            x_round_(0)
            x_round_(1)
            pe.wait_ge(grow_in, 16)
            nc.tensor.transpose(b_p[:, 0:KT], grows, ident[0:KT, 0:KT]).then_inc(crows_T, 1)
            keep_busy(NBUSY)
            for slot in range(LAST):
                unit(slot)
                if slot == 3:
                    pe.wait_ge(crow_in, 64)
                    pe.wait_ge(xg_done, 7)
                    nc.tensor.transpose(b_t[:, 0:80], crows, ident[0:80, 0:80]).then_inc(crows_T, 1)
                if slot in ROUNDS:
                    round_(slot)
                if slot in CK_AT:
                    ck_unit(CK_AT[slot])
                if slot in CK_SUM_SLOT:
                    ck_quarters(CK_SUM_SLOT.index(slot))
                if slot in CK2_SLOT:
                    ck_layer2(CK2_SLOT.index(slot))
                if slot == GATE_SLOT:
                    gates()
                if slot == GATE_SLOT + 1:
                    gate_quarters()
                if slot - 3 in JOB_AT and ends_head(JOB_AT[slot - 3]):
                    values(JOB_AT[slot - 3])
                if slot - 2 in JOB_AT:
                    prob_T(JOB_AT[slot - 2])
                if slot in JOB_AT:
                    scores(JOB_AT[slot])
                for r in Y_ROUNDS.get(slot, []):
                    y_round_(r)
            last_chunk()

        @block.scalar
        def _(act):
            def hi(u):
                act.wait_ge(raw_in[u % RAW], 16 * (u // RAW))
                act.wait_ge(unit_used, u - SPL + 1 if u < NSLOT - 1 else NPROJ)
                nc.scalar.activation(split_of(u)[0], w_raw[:, u % RAW], ACT.Copy).then_inc(hi_ready, 1)

            def first_hi_(u, ks):
                for k in ks:
                    act.wait_ge(first_in[u * UK + k], 16)
                    nc.scalar.activation(w_hi[:, u, k, :], w_raw[:, u, k, :], ACT.Copy).then_inc(first_hi, 1)

            def x_hi(r):
                q, m = r // 2, r % 2
                act.wait_ge(xg_done, r + 1)
                nc.scalar.activation(xT_hi[:, q * UK:(q + 1) * UK, m * P:(m + 1) * P],
                                     x_buf(r), ACT.Copy).then_inc(xhi_done, 1)

            def evac(i):
                kind, _, n = CHUNKS[i]
                act.wait_ge(unit_used, UPC * (i + 1))
                if i == 0:
                    act.wait_ge(rstd_ok, 1)
                if kind == "nq" and n:
                    act.wait_ge(t_round, rounds_by(UPC * i + UPC - 1))
                for m in range(MT):
                    b = proj_b[i % 2][m]
                    if kind in ("kv", "nq"):
                        act.wait_ge(dve_read, dve_reads(i - 1) + 2 * (m + 1))
                    if kind in ("kc", "nq"):
                        nc.scalar.activation(raw_e[:, m, :], b[:, :], ACT.Copy, scale=rstd[:, m:m + 1]).then_inc(act_read, 1)
                    elif kind == "kv":
                        nc.scalar.activation(nv[:, n, m, :], b[:, 2 * HD:4 * HD], ACT.Copy, scale=rstd[:, m:m + 1]).then_inc(act_read, 1)
                    elif kind == "mv":
                        nc.scalar.activation(mv[:, m, n * CW:(n + 1) * CW], b[:, :], ACT.Copy, scale=rstd[:, m:m + 1]).then_inc(act_read, 1)
                    elif kind == "z":
                        z = (rope_a, rope_b)[n % 2]
                        if n >= 2 and m == 0:
                            act.wait_ge(y_done, 2 * (n - 1))
                        if n == 0 and m == 0:
                            act.wait_ge(t_round, len(ROUNDS))
                        nc.scalar.activation(z[:, m, :], b[:, :], ACT.Sigmoid, scale=rstd[:, m:m + 1]).then_inc(act_read, 1)

            def round_out(slot):
                kind, which, _ = ROUNDS[slot]
                if kind == "kc":
                    return
                act.wait_ge(t_round, ROUND_NO[slot] + 1)
                if kind == "kv":
                    dst = Q[:, Q_KS + 2 * which:Q_KS + 2 * which + 2, :]
                    src = b_t[:, :].rearrange("p (g t) -> p g t", g=NG)
                else:
                    n, m = which
                    first = {"rot": Q_ROT + 4 * n, "raw": Q_RAW + 4 * n, "mq": Q_MQ[n], "mk": Q_MK[n]}[kind]
                    dst = Q[:, first:first + HPC, m * P:(m + 1) * P]
                    src = b_t[:, :].rearrange("p (h t) -> p h t", h=HPC)
                nc.scalar.activation(dst, src, ACT.Copy).then_inc(t_out, 1)

            def exps(j):
                act.wait_ge(negmax_ok, j + 1)
                b = j % 2
                for n, (c0, c1) in enumerate(((0, P), (P, 3 * P), (3 * P, 3 * P + NCMP))[:3 if JOBS[j][1] == "nsa" else 2]):
                    last = nc.scalar.activation(prob[:, b, c0:c1], prob[:, b, c0:c1], ACT.Exp, bias=nmx[:, b, n:n + 1],
                                                scale=SCALE, accum_out=sums[:, b, n:n + 1])
                last.then_inc(exp_done, 1)

            def prob_out(j):
                act.wait_ge(pt_done, j + 1)
                last = nc.scalar.activation(pT[:, j % 2, 0:3 * P], b_p[:, 0:3 * P], ACT.Copy)
                if JOBS[j][1] == "nsa":
                    last = nc.scalar.activation(pT[0:NCMP, j % 2, 3 * P:4 * P], b_p[0:NCMP, 3 * P:4 * P], ACT.Copy)
                last.then_inc(pt_out, 1)

            def quarters_out(n):
                act.wait_ge(*((ck_used, 4), (gates_done, 1), (ck_used, 8))[n])
                act.wait_ge(*((cols_ok, 2), (ck_sum, 1), (gates_sum, 1))[n])
                src = (b_s[:, 0:CH], b_o[:, 0:S], b_s[:, CH:2 * CH])[n]
                nc.scalar.activation(quarters, src, ACT.Copy).then_inc(quarters_ok, 1)

            def hidden_exp(kv):
                act.wait_ge(ck_sum, kv + 1)
                nc.scalar.activation(hid_e[:, :, :], b_p[:, 2 * kv * TP:2 * (kv + 1) * TP].rearrange("p (a n) -> p a n", a=2),
                                     ACT.Exp, scale=-1.0).then_inc(ck_exp, 1)

            def ck2_evac(kv):
                act.wait_ge(ck2_done, kv + 1)
                if kv == 0:
                    nc.scalar.activation(kcT[:, 0:TP], b_o[:, 0:TP], ACT.Copy).then_inc(ck2_out, 1)
                else:
                    nc.scalar.activation(vc[0:NCMP, :, :], b_o[0:NCMP, HD:3 * HD].rearrange("p (g d) -> p g d", g=NG),
                                         ACT.Copy).then_inc(ck2_out, 1)

            def y_squares(n):
                for m in range(MT):
                    act.wait_ge(y_done, 2 * n + m + 1)
                    if n + m:
                        act.wait_ge(y_sq, 2 * n + m)
                    nc.scalar.activation(junk[:, 0:CW], xo[:, m, n * CW:(n + 1) * CW], ACT.Square,
                                         accum_out=ssy[:, n // 2, m, n % 2:n % 2 + 1]).then_inc(y_sq, 1)

            def y_hi(r):
                half, hg, m = r
                dst = (ymT_hi, xT_hi)[half]
                act.wait_ge(yg_done, Y_NO[r] + 1)
                nc.scalar.activation(dst[:, hg * HPC:(hg + 1) * HPC, m * P:(m + 1) * P],
                                     pT[:, Y_NO[r] % 2, :].rearrange("p (h t) -> p h t", h=HPC), ACT.Copy).then_inc(yhi_done, 1)

            def final_squares(c, m):
                act.wait_ge(dve_read, dve_reads(NC + c - 1) + m + 1)
                act.wait_ge(*((fin_sq, 2 * c + m) if c + m else (y_sq, 8)))
                nc.scalar.activation(junk[:, 0:CW], acc[:, m, c * CW:(c + 1) * CW], ACT.Square,
                                     accum_out=ssf[:, m, c:c + 1]).then_inc(fin_sq, 1)

            act.dma_start(grows, g_norm[0].rearrange("(k p) -> k p", p=P)).then_inc(grow_in, 16)

            x_hi(0)
            first_hi_(0, [0])
            x_hi(1)
            first_hi_(0, [1, 2, 3])
            for r0, src in ((0, g_out_moba[0].rearrange("(k p) -> k p", p=P)), (8, g_out_nsa[0].rearrange("(k p) -> k p", p=P)),
                            (16, pe_ck[0]), (48, pe_cv[0])):
                act.dma_start(crows[r0:r0 + src.shape[0], :], src).then_inc(crow_in, 16)
            with nc.allow_non_contiguous_dma(reason="256 positions"):
                act.dma_start(pos_i[:, :], positions[0].rearrange("(m p) -> p m", p=P)).then_inc(trig_in, 16)
            act.dma_start(invf[:, :], inv_freq).then_inc(trig_in, 16)
            x_hi(2)
            x_hi(3)
            first_hi_(1, range(UK))
            for slot in range(NSLOT):
                if slot == 0:
                    x_hi(4)
                    x_hi(5)
                    first_hi_(2, range(UK))
                    x_hi(6)
                    x_hi(7)
                elif slot + 2 < NSLOT:
                    hi(slot + 2)
                if slot == 1:
                    with nc.allow_non_contiguous_dma(reason="24 gate columns"):
                        act.dma_start(wg[:, :, :], w_in[0, :, COL_G:COL_G + 32].rearrange("(k p) c -> p k c", p=P)).then_inc(wg_in, 16)
                    for n, w in enumerate((w_ck2, w_cv2)):
                        act.dma_start(w2[:, n, :, :], w[0].rearrange("(t p) d -> p t d", p=P)).then_inc(w2_in, 16)
                if slot == 2:
                    for q in range(5):
                        act.wait_ge(x_in[q], 16)
                    for m in range(MT):
                        if m:
                            act.wait_ge(sq_done, m)
                        nc.scalar.activation(junk, xo[:, m, :], ACT.Square, accum_out=ssx[:, m:m + 1]).then_inc(sq_done, 1)
                if slot in ROUNDS:
                    round_out(slot)
                if slot == 4:
                    act.wait_ge(trig_arg, 2)
                    nc.scalar.activation(trig[:, 2, :], trig[:, 2, :], ACT.Sin).then_inc(trig_act, 1)
                    nc.scalar.activation(trig[:, 3, :], trig[:, 3, :], ACT.Sin).then_inc(trig_act, 1)
                if slot - 1 in JOB_AT:
                    exps(JOB_AT[slot - 1])
                if slot - 2 in JOB_AT:
                    prob_out(JOB_AT[slot - 2])
                if slot % UPC == UPC - 1 and slot < NPROJ and ACT_READS[KINDS[slot // UPC]]:
                    evac(slot // UPC)
                if slot in (CK_SLOT[3], GATE_SLOT, CK_SLOT[7]):
                    quarters_out((CK_SLOT[3], GATE_SLOT, CK_SLOT[7]).index(slot))
                if slot in CK_SUM_SLOT:
                    hidden_exp(CK_SUM_SLOT.index(slot))
                if slot in CK2_SLOT:
                    ck2_evac(CK2_SLOT.index(slot))
                if slot == GATE_SLOT + 1:
                    act.wait_ge(gates_sum, 1)
                    for m in range(MT):
                        nc.scalar.activation(gate[:, m, :], b_o[:, 384 + m * 32:384 + m * 32 + NGATE], ACT.Exp,
                                             scale=nrstd[:, m:m + 1]).then_inc(gate_exp, 1)
                if slot in (49, 52, 56, 60):
                    y_squares((49, 52, 56, 60).index(slot))
                for r in Y_ROUNDS.get(slot, []):
                    y_hi(r)
                if slot in OUT_SLOT:
                    for m in range(MT):
                        final_squares(OUT_SLOT.index(slot), m)
            act.wait_ge(gmul, 4)
            for m in range(MT):
                final_squares(3, m)
                act.wait_ge(rstdf_ok, m + 1)
                nc.scalar.activation(acc[:, m, 0:HW], acc[:, m, 0:HW], ACT.Copy, scale=rstdf[:, m:m + 1]).then_inc(fin_act, 1)

        @block.vector
        def _(dve):
            steps = [0]

            def link(ins):
                steps[0] += 1
                ins.then_inc(dve_step, 1)
                dve.wait_ge(dve_step, steps[0])

            def lo(u):
                dve.wait_ge(hi_ready, u - FIRST + 1)
                wh, wl = split_of(u)
                nc.vector.tensor_tensor(wl, w_raw[:, u % RAW], wh.bitcast(F32), ALU.subtract).then_inc(lo_ready, 1)

            def first_lo_(u, ks):
                for k in ks:
                    dve.wait_ge(first_hi, u * UK + k + 1)
                    nc.vector.tensor_tensor(w_lo[:, u, k, :], w_raw[:, u, k, :], w_hi[:, u, k, :].bitcast(F32),
                                            ALU.subtract).then_inc(first_lo, 1)

            def x_g(r):
                q, m = r // 2, r % 2
                dve.wait_ge(x_round, r + 1)
                if r >= 4:
                    dve.wait_ge((xlo_even, xlo_odd)[m], q - 1)
                g = ccols[:, q * UK:(q + 1) * UK].unsqueeze(2).to_broadcast([P, UK, P])
                nc.vector.tensor_tensor(x_buf(r),
                                        xbanks[r % 4][:, :].rearrange("p (k t) -> p k t", k=UK), g, ALU.mult).then_inc(xg_done, 1)

            def x_lo(r):
                q, m = r // 2, r % 2
                dve.wait_ge(xhi_done, r + 1)
                nc.vector.tensor_tensor(xT_lo[:, q * UK:(q + 1) * UK, m * P:(m + 1) * P],
                                        x_buf(r),
                                        xT_hi[:, q * UK:(q + 1) * UK, m * P:(m + 1) * P].bitcast(F32),
                                        ALU.subtract).then_inc(xlo_odd, 1)

            def angles():
                dve.wait_ge(trig_in, 32)
                link(nc.vector.tensor_copy(pos_f[:, :], pos_i[:, :]))
                ang, n, r, c = (trig[:, i, :] for i in range(4))
                for m in range(MT):
                    link(nc.vector.tensor_scalar(trig[:, 0, m * HALF:(m + 1) * HALF], invf[:, :], pos_f[:, m:m + 1], None, ALU.mult))
                link(nc.vector.tensor_scalar(n, ang, INV_2PI, MAGIC, ALU.mult, ALU.add))
                link(nc.vector.tensor_scalar(n, n, MAGIC, None, ALU.subtract))
                link(nc.vector.scalar_tensor_tensor(r, n, -C1, ang, ALU.mult, ALU.add))
                link(nc.vector.scalar_tensor_tensor(r, n, -C2, r, ALU.mult, ALU.add))
                link(nc.vector.scalar_tensor_tensor(r, n, -C3, r, ALU.mult, ALU.add))
                link(nc.vector.tensor_scalar(r, r, PI, -PI, ALU.min, ALU.max))
                link(nc.vector.scalar_tensor_tensor(c, r, -1.0, r, ALU.mult, ALU.max))
                nc.vector.tensor_scalar(c, c, -1.0, 1.5707963267948966, ALU.mult, ALU.add).then_inc(trig_arg, 2)

            def tables():
                dve.wait_ge(trig_act, 2)
                dve.wait_ge(rstd_ok, 1)
                for m in range(MT):
                    sn, cs = trig[:, 2, m * HALF:(m + 1) * HALF], trig[:, 3, m * HALF:(m + 1) * HALF]
                    nc.vector.tensor_scalar(rope_c[:, m, 0:HALF], cs, rstd[:, m:m + 1], None, ALU.mult).then_inc(tables_ok, 1)
                    nc.vector.tensor_scalar(rope_c[:, m, HALF:HD], cs, rstd[:, m:m + 1], None, ALU.mult).then_inc(tables_ok, 1)
                    nc.vector.tensor_scalar(rope_s[:, m, 0:HALF], sn, rstd[:, m:m + 1], -1.0, ALU.mult, ALU.mult).then_inc(tables_ok, 1)
                    nc.vector.tensor_scalar(rope_s[:, m, HALF:HD], sn, rstd[:, m:m + 1], None, ALU.mult).then_inc(tables_ok, 1)

            def rope(i):
                kind = KINDS[i]
                nh = NG if kind == "kv" else HPC
                dve.wait_ge(unit_used, UPC * (i + 1))
                dve.wait_ge(t_round, rounds_by(UPC * i + UPC - 1))
                dve.wait_ge(rope_sum, rope_sums(i - 1))
                dve.wait_ge(tables_ok, 8)
                for m in range(MT):
                    b = proj_b[i % 2][m][:, 0:nh * HD]
                    heads = b.rearrange("p (h d) -> p h d", h=nh)
                    halves = b.rearrange("p (h a d) -> p h a d", h=nh, a=2)
                    cosb = rope_c[:, m, :].unsqueeze(1).to_broadcast([P, nh, HD])
                    nc.vector.tensor_tensor(rope_a[:, m, 0:nh * HD].rearrange("p (h d) -> p h d", h=nh), heads, cosb,
                                            ALU.mult).then_inc(dve_read, 1)
                    sinb = rope_s[:, m, :].rearrange("p (a d) -> p a d", a=2).unsqueeze(1).to_broadcast([P, nh, 2, HALF])
                    nc.vector.tensor_tensor(rope_b[:, m, 0:nh * HD].rearrange("p (h a d) -> p h a d", h=nh, a=2),
                                            halves[:, :, ::-1, :], sinb, ALU.mult).then_inc(dve_read, 1)

            def kc_out(slot):
                _, m, _ = ROUNDS[slot]
                dve.wait_ge(t_round, ROUND_NO[slot] + 1)
                for kv in range(2):
                    src = b_t[:, kv * 2 * P:(kv + 1) * 2 * P].rearrange("p (a l) -> p a l", l=CS)
                    for half in range(2):
                        pe_ = ccols[:, 32 + kv * CL + half * CS:32 + kv * CL + (half + 1) * CS].unsqueeze(1).unsqueeze(1)
                        dst = kvpe[:, kv, half, :, m * P:(m + 1) * P].rearrange("p g (n l) -> p g n l", l=CS)
                        last = nc.vector.tensor_tensor(dst, src.rearrange("p (g n) l -> p g n l", g=NG),
                                                       pe_.to_broadcast([P, NG, P // CS, CS]), ALU.add)
                last.then_inc(t_out, 1)

            def hidden(kv):
                dve.wait_ge(ck_exp, kv + 1)
                link(nc.vector.tensor_scalar(hid_e[:, :, :], hid_e[:, :, :], 1.0, None, ALU.add))
                link(nc.vector.reciprocal(hid_e[:, :, :], hid_e[:, :, :]))
                nc.vector.tensor_tensor(hidT[:, kv, :, :], b_p[:, 2 * kv * TP:2 * (kv + 1) * TP].rearrange("p (a n) -> p a n", a=2),
                                        hid_e[:, :, :], ALU.mult).then_inc(hid_ready, 1)

            def gates():
                dve.wait_ge(gate_exp, 2)
                link(nc.vector.tensor_scalar(gate[:, :, :], gate[:, :, :], 1.0, None, ALU.add))
                link(nc.vector.reciprocal(gate[:, :, :], gate[:, :, :]))
                v = gate[:, :, :].rearrange("p m (h b) -> p m h b", b=3)
                for b in range(2):
                    for n, (m, br) in enumerate(((0, 1 + b), (1, 1 + b), (b, 0))):
                        last = nc.vector.tensor_copy(gate_j[:, :, b, n], v[:, m, :, br])
                last.then_inc(gates_ok, 1)

            def row_max(j):
                kind, b = JOBS[j][1], JOBS[j][3]
                dve.wait_ge(scores_done, j + 1)
                if j == 0:
                    dve.wait_ge(consts_ok, 4)
                pieces = [(0, P, 0), (P, 3 * P, P)] + ([(3 * P, 3 * P + NCMP, 3 * P + 16 * b)] if kind == "nsa" else [])
                for n, (c0, c1, k0) in enumerate(pieces):
                    nc.vector.tensor_tensor_reduce(out=prob[:, j % 2, c0:c1], in0=b_s[:, c0:c1], in1=mask[:, k0:k0 + c1 - c0],
                                                   scale=1.0, scalar=NEG, op0=ALU.add, op1=ALU.max,
                                                   accum_out=mx[:, j % 2, n:n + 1]).then_inc(s_read, 1)
                dve.wait_ge(s_read, score_reads(j))
                nc.vector.tensor_scalar(nmx[:, j % 2, 0:len(pieces)], mx[:, j % 2, 0:len(pieces)], FLOOR, -SCALE,
                                        ALU.max, ALU.mult).then_inc(negmax_ok, 1)

            def normalise(j):
                _, kind, h, b = JOBS[j]
                n = 3 if kind == "nsa" else 2
                c = coef[:, j % 2, 0:n]
                dve.wait_ge(exp_done, j + 1)
                link(nc.vector.tensor_scalar(c, sums[:, j % 2, 0:n], 1e-30, None, ALU.max))
                link(nc.vector.reciprocal(c, c))
                if kind == "nsa":
                    link(nc.vector.tensor_tensor(c, c, gate_j[:, h, b, 0:3], ALU.mult))
                for i, (c0, c1) in enumerate(((0, P), (P, 3 * P), (3 * P, 3 * P + NCMP))[:n]):
                    last = nc.vector.tensor_scalar(prob[:, j % 2, c0:c1], prob[:, j % 2, c0:c1], coef[:, j % 2, i:i + 1], None, ALU.mult)
                last.then_inc(prob_ready, 1)

            def o_evac(j):
                _, kind, h, _ = JOBS[j]
                col = (0 if kind == "moba" else HW) + h * HD
                dve.wait_ge(pv_done, heads_done(j))
                nc.vector.tensor_copy(xo[:, :, col:col + HD], b_o[:, 0:2 * P].rearrange("p (m d) -> p m d", m=MT)).then_inc(o_out, 1)

            def silu(i):
                n = CHUNKS[i][2]
                z = (rope_a, rope_b)[n % 2]
                for m in range(MT):
                    dve.wait_ge(act_read, act_reads(i - 1) + m + 1)
                    nc.vector.scalar_tensor_tensor(z[:, m, :], proj_b[i % 2][m][:, :], rstd[:, m:m + 1], z[:, m, :],
                                                   ALU.mult, ALU.mult).then_inc(dve_read, 1)

            def y_scale(half):
                dve.wait_ge(rstdy_ok, half + 1)
                for m in range(MT):
                    y = xo[:, m, half * HW:(half + 1) * HW]
                    nc.vector.tensor_scalar(y, y, rstdy[:, half, m:m + 1], None, ALU.mult).then_inc(y_scaled, 1)

            def y_parts(r):
                half, hg, m = r
                n = Y_NO[r]
                bank_ = b_t if half == 0 else (b_t, b_s, b_p, b_o)[n - 4]
                dve.wait_ge(y_round, n + 1)
                dve.wait_ge(pt_out, len(JOBS))
                g0 = 16 + half * NH + hg * HPC
                yg = pT[:, n % 2, :].rearrange("p (h t) -> p h t", h=HPC)
                nc.vector.tensor_tensor(yg, bank_[:, :].rearrange("p (h t) -> p h t", h=HPC),
                                        ccols[:, g0:g0 + HPC].unsqueeze(2).to_broadcast([P, HPC, P]), ALU.mult).then_inc(yg_done, 1)
                dve.wait_ge(yhi_done, n + 1)
                hi_, lo_ = ((ymT_hi, ymT_lo), (xT_hi, xT_lo))[half]
                sl = (slice(None), slice(hg * HPC, (hg + 1) * HPC), slice(m * P, (m + 1) * P))
                nc.vector.tensor_tensor(lo_[sl], yg, hi_[sl].bitcast(F32), ALU.subtract).then_inc(ylo_done, 1)

            def residual(c, m):
                if c == 3:
                    dve.wait_ge(last_done, m + 1)
                else:
                    dve.wait_ge(unit_used, OUT_DONE[c] + 1)
                if c == 0:
                    dve.wait_ge(acc_in, 16)
                a = acc[:, m, c * CW:(c + 1) * CW]
                nc.vector.tensor_tensor(a, proj_b[(NC + c) % 2][m][:, :], a, ALU.add).then_inc(dve_read, 1)

            def row_sum(m):
                dve.wait_ge(fin_sq, 5 + m)
                link(nc.vector.tensor_reduce(ssf1[:, m:m + 1], ssf[:, m, 0:3], mybir.AxisListType.X, ALU.add))
                nc.vector.tensor_scalar(ssf1[:, m:m + 1], ssf1[:, m:m + 1], 1.0 / D, EPS, ALU.mult, ALU.add).then_inc(ssf_ok, 1)

            def final(m):
                dve.wait_ge(rstdf_ok, m + 1)
                r = rstdf[:, m:m + 1]
                nc.vector.tensor_scalar(acc[:, m, 2 * CW:3 * CW], acc[:, m, 2 * CW:3 * CW], r, None, ALU.mult)
                a = acc[:, m, 3 * CW:4 * CW]
                nc.vector.scalar_tensor_tensor(a, a, r, g_fin[:, 3 * CW:4 * CW], ALU.mult, ALU.mult).then_inc(fin_dve, 1)

            dve.wait_ge(crows_T, 1)
            nc.vector.tensor_copy(ccols[:, 0:KT], b_p[:, 0:KT]).then_inc(cols_ok, 1)
            dve.wait_ge(cols_ok, 1)
            x_g(0)
            x_g(1)
            first_lo_(0, [0])
            x_lo(1)
            first_lo_(0, [1, 2, 3])
            x_g(2)
            x_g(3)
            first_lo_(1, [0])
            x_lo(3)
            first_lo_(1, [1, 2, 3])
            for slot in range(NSLOT):
                if slot == 0:
                    x_g(4)
                    x_g(5)
                    first_lo_(2, [0])
                    x_lo(5)
                    x_g(6)
                    x_g(7)
                    first_lo_(2, [1, 2, 3])
                    x_lo(7)
                elif slot + 2 < NSLOT:
                    lo(slot + 2)
                if slot == 3:
                    dve.wait_ge(crows_T, 2)
                    nc.vector.tensor_copy(ccols[:, KT:], b_t[:, 0:80]).then_inc(cols_ok, 1)
                    dve.wait_ge(cols_ok, 2)
                if slot == 2:
                    angles()
                if slot == 5:
                    tables()
                if slot in ROUNDS and ROUNDS[slot][0] == "kc":
                    kc_out(slot)
                if slot - 1 in JOB_AT:
                    normalise(JOB_AT[slot - 1])
                if slot - 3 in JOB_AT and ends_head(JOB_AT[slot - 3]):
                    o_evac(JOB_AT[slot - 3])
                if slot in JOB_AT:
                    row_max(JOB_AT[slot])
                if slot % UPC == UPC - 1 and slot < NPROJ:
                    if KINDS[slot // UPC] in ROPED:
                        rope(slot // UPC)
                    if KINDS[slot // UPC] == "z":
                        silu(slot // UPC)
                if slot in CK_SUM_SLOT:
                    hidden(CK_SUM_SLOT.index(slot))
                if slot == GATE_SLOT + 1:
                    gates()
                if slot in (53, 61):
                    y_scale((53, 61).index(slot))
                for r in Y_ROUNDS.get(slot, []):
                    y_parts(r)
                if slot in OUT_SLOT:
                    for m in range(MT):
                        residual(OUT_SLOT.index(slot), m)
            row_sum(0)
            row_sum(1)
            dve.wait_ge(gmul, 6)
            for m in range(MT):
                residual(3, m)
                final(m)


_INS = ["x", "positions", "inv_freq", "w_in", "g_norm", "pe_ck", "pe_cv", "w_ck1", "w_ck2", "w_cv1", "w_cv2",
        "g_out_moba", "g_out_nsa", "w_out", "g_final"]


def kernel(**inputs):
    import numpy as _np
    import concourse.bacc as _bacc
    from concourse import mybir as _mybir
    from concourse.bass_utils import run_bass_kernel_spmd as _run

    freq = 1.0 / (_np.float32(10000.0) ** (_np.arange(0, HD, 2, dtype=_np.float32) / _np.float32(HD)))
    inv_freq = _np.ascontiguousarray(_np.broadcast_to(freq.astype(_np.float32), (P, HALF)))
    nc = _bacc.Bacc("TRN2", target_bir_lowering=False, num_devices=1)
    arrays, args = {}, []
    for name in _INS:
        a = inv_freq if name == "inv_freq" else _np.ascontiguousarray(inputs[name])
        arrays[f"in_{name}_dram"] = a
        args.append(nc.dram_tensor(f"in_{name}_dram", a.shape, _mybir.dt.from_np(a.dtype), kind="ExternalInput").ap())
    args.append(nc.dram_tensor("out_dram", (1, S, D), _mybir.dt.float32, kind="ExternalOutput").ap())
    build_layer(nc, *args)
    r = _run(nc, [arrays], core_ids=[0])
    return r.results[0]["out_dram"]
```
